# Optimizing a Trainium2 kernel written in Bass

```python
import jax
import jax.numpy as jnp
from jax import lax
import numpy as np

D_MODEL = 1024
BATCH = 1
SEQ = 1024
DEPTH = 2

CHUNK = 64
Q_BLOCK = 128
ROPE_THETA = 10000.0
EPS = 1e-6

MLA_HEADS = 8
MLA_Q_LORA = 256
MLA_KV_LORA = 128
MLA_NOPE = 64
MLA_ROPE = 32
MLA_V = 64

DSA_HEADS = 8
DSA_HEAD_DIM = 64
IDX_HEADS = 8
IDX_DIM = 64
TOPK_MAX = 256

SWA_HEADS = 16
SWA_KV_HEADS = 2
SWA_HEAD_DIM = 64
SWA_WINDOW = 128
SWA_WINDOW_CHUNKS = SWA_WINDOW // CHUNK

D_FF = 2816
CONV_WIDTH = 3

N_EVEN = (DEPTH + 1) // 2
N_ODD = DEPTH // 2

EVEN_SPLITS = (MLA_Q_LORA, MLA_KV_LORA, MLA_ROPE,
               DSA_HEADS * DSA_HEAD_DIM, DSA_HEAD_DIM, DSA_HEAD_DIM,
               IDX_HEADS * IDX_DIM, IDX_DIM, IDX_HEADS)
EVEN_IN = MLA_Q_LORA + MLA_KV_LORA + MLA_ROPE + DSA_HEADS * DSA_HEAD_DIM + 2 * DSA_HEAD_DIM + IDX_HEADS * IDX_DIM + IDX_DIM + IDX_HEADS
EVEN_MIX = MLA_HEADS * MLA_V + DSA_HEADS * DSA_HEAD_DIM
ODD_IN = (SWA_HEADS + 2 * SWA_KV_HEADS) * SWA_HEAD_DIM
ODD_MIX = SWA_HEADS * SWA_HEAD_DIM

kernel_name = "hybrid_mla_dsa_swa_convffn"

def rms_norm(x, g):
    x32 = x.astype(jnp.float32)
    y = x32 * lax.rsqrt(jnp.mean(x32 * x32, axis=-1, keepdims=True) + EPS)
    return (y * g.astype(jnp.float32)).astype(x.dtype)

def rope(x, pos):
    half = x.shape[-1] // 2
    inv_freq = jnp.power(jnp.float32(ROPE_THETA), -jnp.arange(half, dtype=jnp.float32) / half)
    ang = pos.astype(jnp.float32)[:, None] * inv_freq[None, :]
    cos = jnp.cos(ang)[None, :, None, :]
    sin = jnp.sin(ang)[None, :, None, :]
    x32 = x.astype(jnp.float32)
    x1, x2 = x32[..., :half], x32[..., half:]
    return jnp.concatenate([x1 * cos - x2 * sin, x2 * cos + x1 * sin], axis=-1).astype(x.dtype)

def to_blocks(t, size):
    b, s = t.shape[:2]
    return jnp.moveaxis(t.reshape(b, s // size, size, *t.shape[2:]), 1, 0)

def from_blocks(t):
    nb, b, size = t.shape[:3]
    return jnp.moveaxis(t, 0, 1).reshape(b, nb * size, *t.shape[3:])

def dense_chunk_causal_attention(q, k, v, pos):
    s_len = q.shape[1]
    scale = q.shape[-1] ** -0.5
    k_chunk = pos // CHUNK

    def block(args):
        qi, bi = args
        q_chunk = (bi * Q_BLOCK + jnp.arange(Q_BLOCK, dtype=jnp.int32)) // CHUNK
        s = jnp.einsum('bqhd,bkhd->bhqk', qi, k, preferred_element_type=jnp.float32) * scale
        allowed = k_chunk[None, :] <= q_chunk[:, None]
        s = jnp.where(allowed[None, None], s, -jnp.inf)
        p = jax.nn.softmax(s, axis=-1).astype(v.dtype)
        return jnp.einsum('bhqk,bkhd->bqhd', p, v)

    nblk = s_len // Q_BLOCK
    out = lax.map(block, (to_blocks(q, Q_BLOCK), jnp.arange(nblk, dtype=jnp.int32)))
    return from_blocks(out)

def mla_mixer(q_lat, kv_lat, k_rope, qa_norm, w_qb, kva_norm, w_kvb, q_norm, k_norm, pos):
    b, s, _ = q_lat.shape
    q = (rms_norm(q_lat, qa_norm) @ w_qb).reshape(b, s, MLA_HEADS, MLA_NOPE + MLA_ROPE)
    kv = (rms_norm(kv_lat, kva_norm) @ w_kvb).reshape(b, s, MLA_HEADS, MLA_NOPE + MLA_V)
    k_nope, v = kv[..., :MLA_NOPE], kv[..., MLA_NOPE:]
    k_pe = jnp.broadcast_to(k_rope[:, :, None, :], (b, s, MLA_HEADS, MLA_ROPE))
    k = jnp.concatenate([k_nope, k_pe], axis=-1)
    q = rms_norm(q, q_norm)
    k = rms_norm(k, k_norm)
    q = jnp.concatenate([q[..., :MLA_NOPE], rope(q[..., MLA_NOPE:], pos)], axis=-1)
    k = jnp.concatenate([k[..., :MLA_NOPE], rope(k[..., MLA_NOPE:], pos)], axis=-1)
    return dense_chunk_causal_attention(q, k, v, pos)

def dsa_mixer(q, k, v, q_idx, k_idx, w_idx, q_norm, k_norm, idx_k_norm, pos):
    b, s, _ = q.shape
    topk = min(TOPK_MAX, s // 4)
    scale = DSA_HEAD_DIM ** -0.5
    q = rope(rms_norm(q.reshape(b, s, DSA_HEADS, DSA_HEAD_DIM), q_norm), pos)
    k = rope(rms_norm(k, k_norm)[:, :, None, :], pos)[:, :, 0, :]
    q_idx = rope(q_idx.reshape(b, s, IDX_HEADS, IDX_DIM), pos)
    k_idx = rope(rms_norm(k_idx, idx_k_norm)[:, :, None, :], pos)[:, :, 0, :]
    w_idx = w_idx.astype(jnp.float32) * (IDX_HEADS ** -0.5 * IDX_DIM ** -0.5)
    k_chunk = pos // CHUNK

    def block(args):
        qi, qii, wi, bi = args
        q_chunk = (bi * Q_BLOCK + jnp.arange(Q_BLOCK, dtype=jnp.int32)) // CHUNK
        dots = jnp.einsum('bqhd,bsd->bqhs', qii, k_idx, preferred_element_type=jnp.float32)
        score = jnp.einsum('bqhs,bqh->bqs', jax.nn.relu(dots), wi)
        visible = k_chunk[None, :] <= q_chunk[:, None]
        score = jnp.where(visible[None], score, -jnp.inf)
        _, idx = lax.top_k(score, topk)
        valid = (idx // CHUNK) <= q_chunk[None, :, None]
        k_sel = jax.vmap(lambda kb, ib: kb[ib])(k, idx)
        v_sel = jax.vmap(lambda vb, ib: vb[ib])(v, idx)
        sc = jnp.einsum('bqhd,bqkd->bhqk', qi, k_sel, preferred_element_type=jnp.float32) * scale
        sc = jnp.where(valid[:, None], sc, -jnp.inf)
        p = jax.nn.softmax(sc, axis=-1).astype(v.dtype)
        return jnp.einsum('bhqk,bqkd->bqhd', p, v_sel)

    nblk = s // Q_BLOCK
    out = lax.map(block, (to_blocks(q, Q_BLOCK), to_blocks(q_idx, Q_BLOCK),
                          to_blocks(w_idx, Q_BLOCK), jnp.arange(nblk, dtype=jnp.int32)))
    return from_blocks(out)

def swa_mixer(q, k, v, q_norm, k_norm, sinks, pos):
    b, s, _ = q.shape
    g = SWA_HEADS // SWA_KV_HEADS
    w = SWA_WINDOW_CHUNKS
    n_chunks = s // CHUNK
    scale = SWA_HEAD_DIM ** -0.5
    q = rope(rms_norm(q.reshape(b, s, SWA_HEADS, SWA_HEAD_DIM), q_norm), pos)
    k = rope(rms_norm(k.reshape(b, s, SWA_KV_HEADS, SWA_HEAD_DIM), k_norm), pos)
    v = v.reshape(b, s, SWA_KV_HEADS, SWA_HEAD_DIM)
    qc = q.reshape(b, n_chunks, CHUNK, SWA_KV_HEADS, g, SWA_HEAD_DIM)

    def band(t):
        tc = t.reshape(b, n_chunks, CHUNK, SWA_KV_HEADS, SWA_HEAD_DIM)
        padded = jnp.pad(tc, ((0, 0), (w - 1, 0), (0, 0), (0, 0), (0, 0)))
        return jnp.concatenate([padded[:, j:j + n_chunks] for j in range(w)], axis=2)

    kb, vb = band(k), band(v)
    chunk_id = jnp.arange(n_chunks, dtype=jnp.int32)
    slot = jnp.arange(w * CHUNK, dtype=jnp.int32) // CHUNK
    valid = (chunk_id[:, None] - (w - 1) + slot[None, :]) >= 0
    sc = jnp.einsum('bcqkgd,bcskd->bckgqs', qc, kb, preferred_element_type=jnp.float32) * scale
    sc = jnp.where(valid[None, :, None, None, None, :], sc, -jnp.inf)
    sink = jnp.broadcast_to(sinks.astype(jnp.float32).reshape(1, 1, SWA_KV_HEADS, g, 1, 1),
                            sc.shape[:-1] + (1,))
    p = jax.nn.softmax(jnp.concatenate([sc, sink], axis=-1), axis=-1)[..., :-1].astype(v.dtype)
    out = jnp.einsum('bckgqs,bcskd->bcqkgd', p, vb)
    return out.reshape(b, s, SWA_HEADS * SWA_HEAD_DIM)

def conv_ffn(x, g, w_up, conv_w, conv_b, w_down):
    s = x.shape[1]
    h = rms_norm(x, g) @ w_up
    hp = jnp.pad(h, ((0, 0), (CONV_WIDTH - 1, 0), (0, 0)))
    acc = conv_b
    for j in range(CONV_WIDTH):
        acc = acc + conv_w[j] * hp[:, j:j + s]
    gate, up = jnp.split(acc, 2, axis=-1)
    return (jax.nn.silu(gate) * up) @ w_down

def setup_inputs(seed: int = 0) -> dict:
    key = jax.random.key(seed)
    ks = iter(jax.random.split(key, 32))

    def normal(shape, scale):
        return scale * jax.random.normal(next(ks), shape, jnp.float32)

    def gain(shape):
        return 1.0 + 0.02 * jax.random.normal(next(ks), shape, jnp.float32)

    return {
        "x": normal((BATCH, SEQ, D_MODEL), 1.0),
        "e_norm": gain((N_EVEN, D_MODEL)),
        "e_w_in": normal((N_EVEN, D_MODEL, EVEN_IN), D_MODEL ** -0.5),
        "e_qa_norm": gain((N_EVEN, MLA_Q_LORA)),
        "e_w_qb": normal((N_EVEN, MLA_Q_LORA, MLA_HEADS * (MLA_NOPE + MLA_ROPE)), MLA_Q_LORA ** -0.5),
        "e_kva_norm": gain((N_EVEN, MLA_KV_LORA)),
        "e_w_kvb": normal((N_EVEN, MLA_KV_LORA, MLA_HEADS * (MLA_NOPE + MLA_V)), MLA_KV_LORA ** -0.5),
        "e_mla_qnorm": gain((N_EVEN, MLA_NOPE + MLA_ROPE)),
        "e_mla_knorm": gain((N_EVEN, MLA_NOPE + MLA_ROPE)),
        "e_dsa_qnorm": gain((N_EVEN, DSA_HEAD_DIM)),
        "e_dsa_knorm": gain((N_EVEN, DSA_HEAD_DIM)),
        "e_idx_knorm": gain((N_EVEN, IDX_DIM)),
        "e_w_out": normal((N_EVEN, EVEN_MIX, D_MODEL), EVEN_MIX ** -0.5),
        "o_norm": gain((N_ODD, D_MODEL)),
        "o_w_in": normal((N_ODD, D_MODEL, ODD_IN), D_MODEL ** -0.5),
        "o_qnorm": gain((N_ODD, SWA_HEAD_DIM)),
        "o_knorm": gain((N_ODD, SWA_HEAD_DIM)),
        "o_sinks": normal((N_ODD, SWA_HEADS), 0.5),
        "o_w_out": normal((N_ODD, ODD_MIX, D_MODEL), ODD_MIX ** -0.5),
        "f_norm": gain((DEPTH, D_MODEL)),
        "f_w_up": normal((DEPTH, D_MODEL, 2 * D_FF), D_MODEL ** -0.5),
        "f_conv_w": normal((DEPTH, CONV_WIDTH, 2 * D_FF), CONV_WIDTH ** -0.5),
        "f_conv_b": normal((DEPTH, 2 * D_FF), 0.01),
        "f_w_down": normal((DEPTH, D_FF, D_MODEL), D_FF ** -0.5),
    }

def reference(x, e_norm, e_w_in, e_qa_norm, e_w_qb, e_kva_norm, e_w_kvb, e_mla_qnorm,
              e_mla_knorm, e_dsa_qnorm, e_dsa_knorm, e_idx_knorm, e_w_out,
              o_norm, o_w_in, o_qnorm, o_knorm, o_sinks, o_w_out,
              f_norm, f_w_up, f_conv_w, f_conv_b, f_w_down):
    b, s, _ = x.shape
    pos = jnp.arange(s, dtype=jnp.int32)
    even_points = [int(p) for p in np.cumsum(EVEN_SPLITS)[:-1]]
    odd_points = [SWA_HEADS * SWA_HEAD_DIM, (SWA_HEADS + SWA_KV_HEADS) * SWA_HEAD_DIM]
    for layer in range(DEPTH):
        i = layer // 2
        if layer % 2 == 0:
            h = rms_norm(x, e_norm[i]) @ e_w_in[i]
            q_lat, kv_lat, k_rope, bq, bk, bv, iq, ik, iw = jnp.split(h, even_points, axis=-1)
            a_out = mla_mixer(q_lat, kv_lat, k_rope, e_qa_norm[i], e_w_qb[i], e_kva_norm[i],
                              e_w_kvb[i], e_mla_qnorm[i], e_mla_knorm[i], pos)
            b_out = dsa_mixer(bq, bk, bv, iq, ik, iw, e_dsa_qnorm[i], e_dsa_knorm[i],
                              e_idx_knorm[i], pos)
            mix = jnp.concatenate([a_out.reshape(b, s, MLA_HEADS * MLA_V),
                                   b_out.reshape(b, s, DSA_HEADS * DSA_HEAD_DIM)], axis=-1)
            x = x + mix @ e_w_out[i]
        else:
            h = rms_norm(x, o_norm[i]) @ o_w_in[i]
            q, k, v = jnp.split(h, odd_points, axis=-1)
            x = x + swa_mixer(q, k, v, o_qnorm[i], o_knorm[i], o_sinks[i], pos) @ o_w_out[i]
        x = x + conv_ffn(x, f_norm[layer], f_w_up[layer], f_conv_w[layer], f_conv_b[layer],
                         f_w_down[layer])
    return x


_drawn_inputs = setup_inputs


def setup_inputs(seed=0):
    import zlib

    import numpy as np

    out = dict(_drawn_inputs(seed))
    spreads = {}
    factors = {'e_norm': 4.392,
     'e_qa_norm': 8.0,
     'e_kva_norm': 8.0,
     'e_mla_qnorm': 8.0,
     'e_mla_knorm': 8.0,
     'e_dsa_qnorm': 8.0,
     'e_dsa_knorm': 8.0,
     'e_idx_knorm': 6.329,
     'o_norm': 8.0,
     'o_qnorm': 8.0,
     'o_knorm': 8.0,
     'o_sinks': 8.0,
     'f_norm': 2.69,
     'f_conv_b': 5.444}
    for name, (base, spread) in spreads.items():
        noise = np.random.default_rng([zlib.crc32(name.encode()), seed]).standard_normal(out[name].shape)
        drawn = base * np.exp(spread * noise) if base else spread * noise
        out[name] = jnp.asarray(drawn.astype(out[name].dtype))
    for name, factor in factors.items():
        out[name] = (out[name] * factor).astype(out[name].dtype)
    return out
```

```python
from contextlib import ExitStack

import numpy as np

import concourse.bass as bass
from concourse import mybir

F32 = mybir.dt.float32
F32R = mybir.dt.float32r
ACT = mybir.ActivationFunctionType
ALU = mybir.AluOpType
AX = mybir.AxisListType
ds = bass.ds

P = 128
S = 1024
DEPTH = 2
D = 1024
SB = S // P
DC = D // P
HALF = 512
EPS = 1e-6
D_FF = 2816
FC = D_FF // P
COL_E_NORM = 0
COL_O_NORM = DC
COL_F_NORM = 2 * DC
COL_CONV_B = 4 * DC
COL_CONV_W = COL_CONV_B + 2 * 2 * FC
N_COLS = COL_CONV_W + 2 * 3 * 2 * FC


class Core:

    def __init__(self, nc, stack):
        self.nc, self.stack = nc, stack
        sb = self.sbuf
        self.xT = sb("xT", [P, DC, S])
        self.cols = sb("cols", [P, N_COLS])
        self.ident = sb("ident", [P, P])
        self.stored = [stack.enter_context(nc.semaphore(f"stored{i}")) for i in range(2)]
        self.ones = sb("ones", [P, P])
        self.minus_half = sb("minus_half", [P, 2 * SB])
        self.rstd = sb("rstd", [P, SB])

    def sbuf(self, name, shape, dtype=F32):
        return self.stack.enter_context(self.nc.sbuf_tensor(name, shape, dtype))


class Phase:

    retired = []

    def __init__(self, nc, tag):
        self.nc, self.tag, self.stack = nc, tag, ExitStack()
        self.free, self.sems = None, []

    def borrow(self, tile):
        self.free = tile

    def sbuf(self, name, shape, dtype=F32):
        n = int(np.prod(shape[1:]))
        if self.free is not None and shape[0] == P and n <= self.free.shape[1]:
            out, self.free = self.free[:, 0:n], self.free[:, n:]
            if dtype != F32:
                out = out.bitcast(dtype)
            names = "abcd"[:len(shape) - 1]
            return out.rearrange(f"p ({' '.join(names)}) -> p {' '.join(names)}", **dict(zip(names, shape[1:])))
        return self.stack.enter_context(self.nc.sbuf_tensor(f"{self.tag}_{name}", shape, dtype))

    def product_sbuf(self, name, shape):
        return self.stack.enter_context(self.nc.sbuf_tensor(f"{self.tag}_{name}", shape, F32R))

    def psum(self, name, columns):
        return self.stack.enter_context(self.nc.psum_tensor(f"{self.tag}_{name}", [P, columns], F32))

    def sem(self, name):
        self.sems.append(self.nc.alloc_semaphore(name=f"{self.tag}_{name}"))
        return self.sems[-1]

    def __enter__(self):
        return self

    def __exit__(self, kind, *error):
        if self.sems and kind is None:
            if Phase.retired:
                self.nc.clear_and_free_semaphores(Phase.retired)
            self.nc.all_engine_barrier()
            Phase.retired = self.sems
        return self.stack.__exit__(kind, *error)


def split_matmuls(pe, out, w_hi, w_lo, x_hi, x_lo, first, last):
    pe.matmul(out, w_hi, x_hi, start=first, stop=False)
    pe.matmul(out, w_hi, x_lo, start=False, stop=False)
    return pe.matmul(out, w_lo, x_hi, start=False, stop=last)


class SquareSum:

    def __init__(self, core, ph, sum_psum, square, total):
        self.core, self.psum, self.square, self.total = core, sum_psum, square, total
        self.mean = ph.sbuf("square_mean", [P, SB])
        self.squared, self.added, self.summed = ph.sem("squared"), ph.sem("squares_added"), ph.sem("summed")
        self.averaged, self.rooted = ph.sem("squares_averaged"), ph.sem("token_roots")

    def scalar(self, act, c, chunk_done, value):
        act.wait_ge(chunk_done, value)
        if c >= 2:
            act.wait_ge(self.added, c - 1)
        act.activation(self.square[:, c % 2], self.core.xT[:, c, :], ACT.Square).then_inc(self.squared, 1)

    def vector(self, dve, c):
        dve.wait_ge(self.squared, c + 1)
        if c == 0:
            dve.tensor_copy(self.total, self.square[:, 0]).then_inc(self.added, 1)
        else:
            dve.wait_ge(self.added, c)
            dve.tensor_tensor(self.total, self.total, self.square[:, c % 2], ALU.add).then_inc(self.added, 1)

    def tensor(self, pe):
        pe.wait_ge(self.added, DC)
        for b in range(SB):
            ins = pe.matmul(self.psum[:, b:b + 1], self.total[:, b * P:(b + 1) * P], self.core.ones[:, 0:1],
                            start=True, stop=True)
        ins.then_inc(self.summed, 1)

    def average(self, dve):
        dve.wait_ge(self.summed, 1)
        dve.tensor_scalar(self.mean[:, :], self.psum[:, 0:SB], 1.0 / D, EPS, ALU.mult, ALU.add)\
           .then_inc(self.averaged, 1)

    def gpsimd(self, pool):
        pool.wait_ge(self.averaged, 1)
        pool.tensor_tensor(self.core.rstd[:, :], self.mean[:, :], self.core.minus_half[:, 0:SB], ALU.pow)\
            .then_inc(self.rooted, 1)


class Norm:

    UNITS = 2 * DC

    def __init__(self, core, ph, gain_column, rstd_psum):
        self.core, self.gain, self.rstd_psum = core, gain_column, rstd_psum
        self.hi = ph.sbuf("xn_hi", [P, DC, S], F32R)
        self.lo = ph.sbuf("xn_lo", [P, DC, S], F32R)
        self.diagonal, self.spread, self.scaled, self.hi_done = (
            ph.sem("diagonal"), ph.sem("spread"), ph.sem("scaled"), ph.sem("xn_hi_done"))
        self.by_vector, self.by_gpsimd = ph.sem("xn_lo_by_vector"), ph.sem("xn_lo_by_gpsimd")

    def buffers(self, work):
        self.diag = work[:, 0:S]
        self.scaled_x = work[:, S:3 * S].rearrange("p (b s) -> p b s", b=4)

    def at(self, n):
        return n % DC, slice(n // DC * HALF, (n // DC + 1) * HALF)

    def wait_lo(self, eng, n):
        eng.wait_ge(self.by_vector, n // 2 + 1)
        if n:
            eng.wait_ge(self.by_gpsimd, (n + 1) // 2)

    def scalar(self, act, after=lambda n: None):
        for n in range(self.UNITS):
            c, t = self.at(n)
            act.wait_ge(self.scaled, n + 1)
            act.activation(self.hi[:, c, t], self.scaled_x[:, n % 4], ACT.Copy).then_inc(self.hi_done, 1)
            after(n)

    def rest(self, eng, n, done):
        c, t = self.at(n)
        eng.wait_ge(self.hi_done, n + 1)
        eng.tensor_tensor(self.lo[:, c, t], self.scaled_x[:, n % 4], self.hi[:, c, t].bitcast(F32), ALU.subtract)\
           .then_inc(done, 1)

    def gpsimd(self, pool, after=lambda n: None):
        for n in range(1, self.UNITS, 2):
            self.rest(pool, n, self.by_gpsimd)
            after(n)

    def vector(self, dve, after=lambda n: None):
        for h in range(2):
            for b in range(h * SB // 2, (h + 1) * SB // 2):
                ins = dve.tensor_scalar(self.diag[:, b * P:(b + 1) * P], self.core.ident[:, :],
                                        self.core.rstd[:, b:b + 1], None, ALU.mult)
            ins.then_inc(self.diagonal, 1)
        after(-1)
        for n in range(self.UNITS + 2):
            if n < self.UNITS:
                c, t = self.at(n)
                if c == 0:
                    dve.wait_ge(self.spread, n // DC + 1)
                if n >= 4:
                    self.wait_lo(dve, n - 4)
                g = self.gain + c
                dve.scalar_tensor_tensor(self.scaled_x[:, n % 4], self.core.xT[:, c, t], self.core.cols[:, g:g + 1],
                                         self.rstd_psum[:, t], ALU.mult, ALU.mult).then_inc(self.scaled, 1)
                after(n)
            if n >= 2 and n % 2 == 0:
                self.rest(dve, n - 2, self.by_vector)

    def tensor(self, pe):
        for h in range(2):
            pe.wait_ge(self.diagonal, h + 1)
            pe.matmul(self.rstd_psum[:, h * HALF:(h + 1) * HALF], self.core.ones[:, :],
                      self.diag[:, h * HALF:(h + 1) * HALF], start=True, stop=True).then_inc(self.spread, 1)


def load(core, x, cols, ident):
    nc = core.nc
    ROWS = N_COLS // P
    with Phase(nc, "load") as ph:
        x_in = ph.sbuf("x_in", [P, 4, D])
        rows = ph.sbuf("rows", [P, ROWS, P])
        turned = [ph.psum(f"turned{i}", S) for i in range(4)]
        squares, square_sum = ph.sbuf("squares", [P, D]), ph.sbuf("square_sum", [P, 2, SB])
        squared, averaged, rooted = ph.sem("squared"), ph.sem("averaged"), ph.sem("rooted")
        x_ready = [ph.sem(f"x_ready{i}") for i in range(4)]
        rows_ready, ident_ready, ones_ready = ph.sem("rows_ready"), ph.sem("ident_ready"), ph.sem("ones_ready")
        turns, rows_turned, rows_copied = ph.sem("turns"), ph.sem("rows_turned"), ph.sem("rows_copied")
        low_copied, high_copied = ph.sem("low_copied"), ph.sem("high_copied")
        with nc.Block() as block:
            @block.sync
            def _(sp):
                sp.dma_start(core.ident[:, :], ident).then_inc(ident_ready, 16)
                for b in range(SB):
                    if b >= 4:
                        sp.wait_ge(turns, b - 3)
                        sp.wait_ge(squared, b - 3)
                    sp.dma_start(x_in[:, b % 4, :], x[b * P:(b + 1) * P, :]).then_inc(x_ready[b % 4], 16)

            @block.scalar
            def _(act):
                at = 0
                for rows_dram in cols:
                    n = rows_dram.shape[0]
                    done = 0
                    while done < n:
                        k = min(n - done, P - at % P)
                        act.dma_start(rows[at % P:at % P + k, at // P, :], rows_dram[done:done + k, :])\
                           .then_inc(rows_ready, 16)
                        at += k
                        done += k
                for b in range(SB):
                    act.wait_ge(x_ready[b % 4], 16 * (b // 4 + 1))
                    if b:
                        act.wait_ge(squared, b)
                    act.activation(squares[:, :], x_in[:, b % 4, :], ACT.Square, accum_out=square_sum[:, 0, b:b + 1])\
                       .then_inc(squared, 1)
                    act.wait_ge(turns, b + 1)
                    act.activation(core.xT[:, 4:8, b * P:(b + 1) * P],
                                   turned[b % 4][:, HALF:].rearrange("p (c s) -> p c s", c=4), ACT.Copy)\
                       .then_inc(high_copied, 1)

            @block.vector
            def _(dve):
                dve.memset(core.ones[:, :], 1.0).then_inc(ones_ready, 1)
                dve.memset(core.minus_half[:, :], -0.5).then_inc(ones_ready, 1)
                for b in range(SB):
                    dve.wait_ge(turns, b + 1)
                    dve.tensor_copy(core.xT[:, 0:4, b * P:(b + 1) * P],
                                    turned[b % 4][:, 0:HALF].rearrange("p (c s) -> p c s", c=4))\
                       .then_inc(low_copied, 1)
                dve.wait_ge(rows_turned, 1)
                dve.tensor_copy(core.cols[:, :], turned[0][:, 0:N_COLS]).then_inc(rows_copied, 1)
                dve.wait_ge(squared, SB)
                dve.tensor_scalar(square_sum[:, 1, :], square_sum[:, 0, :], 1.0 / D, EPS, ALU.mult, ALU.add)\
                   .then_inc(averaged, 1)

            @block.gpsimd
            def _(pool):
                pool.wait_ge(averaged, 1)
                pool.wait_ge(ones_ready, 2)
                pool.tensor_tensor(core.rstd[:, :], square_sum[:, 1, :], core.minus_half[:, 0:SB], ALU.pow)\
                    .then_inc(rooted, 1)

            @block.tensor
            def _(pe):
                pe.wait_ge(ident_ready, 16)
                for b in range(SB):
                    pe.wait_ge(x_ready[b % 4], 16 * (b // 4 + 1))
                    if b >= 4:
                        pe.wait_ge(low_copied, b - 3)
                        pe.wait_ge(high_copied, b - 3)
                    for c in range(DC):
                        ins = pe.transpose(turned[b % 4][:, c * P:(c + 1) * P], x_in[:, b % 4, c * P:(c + 1) * P],
                                           core.ident[:, :])
                    ins.then_inc(turns, 1)
                pe.wait_ge(rows_ready, 16 * 7)
                pe.wait_ge(low_copied, 5)
                pe.wait_ge(high_copied, 5)
                for t in range(ROWS):
                    ins = pe.transpose(turned[0][:, t * P:(t + 1) * P], rows[:, t, :], core.ident[:, :])
                ins.then_inc(rows_turned, 1)


def conv_ffn(core, layer, w_up, w_down, out=None):
    nc = core.nc
    PAIRS = FC // 2
    with Phase(nc, f"ffn{layer}") as ph:
        gate_psum, up_psum = ph.psum("gate_psum", S), ph.psum("up_psum", S)
        y_psum = [ph.psum(f"y_psum{i}", S) for i in range(2)]
        norm = Norm(core, ph, COL_F_NORM + layer * DC, y_psum[1])
        act_hi = ph.sbuf("act_hi", [P, 2, S], F32R)
        act_lo = ph.sbuf("act_lo", [P, 2, S], F32R)
        work = ph.sbuf("work", [P, 4 * S])
        norm.buffers(work)
        if out is not None:
            y_nat = work[:, 0:2 * S].rearrange("p (k b n) -> p k b n", k=2, b=SB)
            out_turned, out_copied = ph.sem("out_turned"), ph.sem("out_copied")
            out_psum = [gate_psum, up_psum]
            out_view = out.rearrange("(b p) n -> p b n", p=P)
        else:
            squares = SquareSum(core, ph, up_psum, work[:, 0:2 * S].rearrange("p (b s) -> p b s", b=2),
                                work[:, 2 * S:3 * S])
        gate_acc, up_acc, silu, act = (work[:, i * S:(i + 1) * S] for i in range(4))
        raw = {n: ph.sbuf(f"{n}_raw", [P, k, D]) for n, k in (("gate", 1), ("up", 1), ("down", 2))}
        hi = {n: ph.sbuf(f"{n}_hi", [P, k, D], F32R) for n, k in (("gate", 1), ("up", 1), ("down", 2))}
        lo = {n: ph.sbuf(f"{n}_lo", [P, k, D], F32R) for n, k in (("gate", 1), ("up", 1), ("down", 2))}
        loaded = {n: ph.sem(f"{n}_loaded") for n in raw}
        hi_done = {n: ph.sem(f"{n}_hi_done") for n in raw}
        lo_done = {n: ph.sem(f"{n}_lo_done") for n in raw}
        product = {n: ph.sem(f"{n}_product") for n in raw}
        tap2 = {n: ph.sem(f"{n}_tap2") for n in ("gate", "up")}
        tap1 = {n: ph.sem(f"{n}_tap1") for n in ("gate", "up")}
        conv = {n: ph.sem(f"{n}_conv") for n in ("gate", "up")}
        gated, multiplied = ph.sem("gated"), ph.sem("multiplied")
        act_hi_done, act_lo_done = ph.sem("act_hi_done"), ph.sem("act_lo_done")
        y_ready, y_added = ph.sem("y_ready"), ph.sem("y_added")
        cols = core.cols
        acc = {"gate": gate_acc, "up": up_acc}
        pre = {"gate": gate_psum, "up": up_psum}
        first_column = {"gate": 0, "up": FC}
        up_view = w_up.rearrange("(c p) n -> p c n", p=P)
        down_view = w_down.rearrange("(f p) n -> p f n", p=P)

        def tap(n, j, k):
            at = COL_CONV_W + (layer * 3 + j) * 2 * FC + first_column[n]
            return cols[:, ds(at + k, 1)]

        def bias(n, k):
            return cols[:, ds(COL_CONV_B + layer * 2 * FC + first_column[n] + k, 1)]

        with nc.Block() as block:
            @block.sync
            def _(sp):
                def load_up(n, k, first=False):
                    if not first:
                        sp.wait_ge(lo_done[n], k)
                    sp.dma_start(raw[n][:, 0, :].rearrange("p (c n) -> p c n", c=DC),
                                 up_view[:, :, ds(first_column[n] * P + k * P, P)]).then_inc(loaded[n], 16)

                def load_down(i, first=False):
                    if not first:
                        sp.wait_ge(lo_done["down"], i)
                    sp.dma_start(raw["down"][:, :, :], down_view[:, ds(2 * i, 2), :]).then_inc(loaded["down"], 16)

                load_up("gate", 0, True)
                load_up("up", 0, True)
                load_up("gate", 1)
                load_down(0, True)
                load_up("up", 1)
                with sp.Fori(1, PAIRS) as i:
                    load_up("gate", 2 * i)
                    load_up("up", 2 * i)
                    load_up("gate", 2 * i + 1)
                    load_down(i)
                    load_up("up", 2 * i + 1)
                if out is not None:
                    for c in range(DC):
                        sp.wait_ge(out_copied, c + 1)
                        sp.dma_start(out_view[:, :, c * P:(c + 1) * P], y_nat[:, c % 2]).then_inc(core.stored[c % 2], 16)
                    for c in range(2):
                        sp.wait_ge(core.stored[c], 16 * DC // 2)

            @block.tensor
            def _(pe):
                def half_product(n, h, first=False):
                    t = slice(h * HALF, (h + 1) * HALF)
                    for c in range(DC):
                        if first:
                            norm.wait_lo(pe, h * DC + c)
                        w = slice(c * P, (c + 1) * P)
                        ins = split_matmuls(pe, pre[n][:, t], hi[n][:, 0, w], lo[n][:, 0, w],
                                            norm.hi[:, c, t], norm.lo[:, c, t], c == 0, c == DC - 1)
                    return ins

                def up_product(n, k):
                    pe.wait_ge(lo_done[n], k + 1)
                    pe.wait_ge(conv[n], k)
                    for h in range(2):
                        ins = half_product(n, h)
                    ins.then_inc(product[n], 1)

                def down_part(c, f):
                    w = slice(c * P, (c + 1) * P)
                    for h in range(2):
                        t = slice(h * HALF, (h + 1) * HALF)
                        ins = split_matmuls(pe, y_psum[c % 2][:, t], hi["down"][:, f, w], lo["down"][:, f, w],
                                            act_hi[:, f, t], act_lo[:, f, t], f == 0, f == 1)
                    return ins

                def down_product(i, behind=lambda c: None, first=False, last=False):
                    pe.wait_ge(lo_done["down"], i + 1)
                    if last:
                        pe.wait_ge(act_lo_done, 2 * i + 1)
                        for c in range(2):
                            pe.wait_ge(y_added, DC * i + c - 1)
                            down_part(c, 0)
                    pe.wait_ge(act_lo_done, 2 * i + 2)
                    for c in range(DC):
                        if not (last and c < 2):
                            if not (first and c < 2):
                                pe.wait_ge(y_added, DC * i + c - 1)
                            down_part(c, 0)
                        down_part(c, 1).then_inc(y_ready, 1)
                        behind(c)

                def turn_output(c):
                    pe.wait_ge(y_added, DC * (PAIRS - 1) + c + 1)
                    if c >= 2:
                        pe.wait_ge(out_copied, c - 1)
                    for b in range(SB):
                        ins = pe.transpose(out_psum[c % 2][:, b * P:(b + 1) * P], core.xT[:, c, b * P:(b + 1) * P],
                                           core.ident[:, :])
                    ins.then_inc(out_turned, 1)

                norm.tensor(pe)
                for h in range(2):
                    for n in ("gate", "up"):
                        if h == 0:
                            pe.wait_ge(lo_done[n], 1)
                        ins = half_product(n, h, n == "gate")
                        if h == 1:
                            ins.then_inc(product[n], 1)
                up_product("gate", 1)
                up_product("up", 1)
                up_product("gate", 2)
                down_product(0, first=True)
                up_product("up", 2)
                up_product("gate", 3)
                up_product("up", 3)
                with pe.Fori(2, PAIRS) as i:
                    up_product("gate", 2 * i)
                    down_product(i - 1)
                    up_product("up", 2 * i)
                    up_product("gate", 2 * i + 1)
                    up_product("up", 2 * i + 1)
                if out is None:
                    down_product(PAIRS - 1, last=True)
                    squares.tensor(pe)
                else:
                    down_product(PAIRS - 1, lambda c: turn_output(c - 1) if c else None, last=True)
                    turn_output(DC - 1)

            @block.scalar
            def _(act_):
                def split_hi(n, k, first=False):
                    act_.wait_ge(loaded[n], 16 * k + 16)
                    if not first:
                        act_.wait_ge(*((y_ready, DC * k) if n == "down" else (product[n], k)))
                    act_.activation(hi[n][:, :, :], raw[n][:, :, :], ACT.Copy).then_inc(hi_done[n], 1)

                def last_tap(n, k, first=False):
                    act_.wait_ge(product[n], k + 1)
                    if not first:
                        act_.wait_ge(multiplied, k)
                    if first:
                        norm.wait_lo(act_, norm.UNITS - 1)
                    act_.activation(acc[n], pre[n][:, :], ACT.Identity, bias=bias(n, k), scale=tap(n, 2, k))\
                        .then_inc(tap2[n], 1)

                def gate(k):
                    act_.wait_ge(conv["gate"], k + 1)
                    act_.activation(silu, gate_acc, ACT.Silu).then_inc(gated, 1)

                def chunk(k, i, slot, first=False, last=False, first_pair=False):
                    last_tap("gate", k, first)
                    if not last:
                        split_hi("gate", k + 1)
                    if slot == 0:
                        split_hi("down", i, first_pair)
                    gate(k)
                    last_tap("up", k, first)
                    if not last:
                        split_hi("up", k + 1)
                    act_.wait_ge(multiplied, k + 1)
                    if slot == 0 and not first_pair:
                        act_.wait_ge(y_ready, DC * i)
                    act_.activation(act_hi[:, slot, :], act, ACT.Copy).then_inc(act_hi_done, 1)

                split_hi("gate", 0, True)
                split_hi("up", 0, True)
                norm.scalar(act_)
                chunk(0, 0, 0, first=True, first_pair=True)
                chunk(1, 0, 1)
                with act_.Fori(1, PAIRS - 1) as i:
                    chunk(2 * i, i, 0)
                    chunk(2 * i + 1, i, 1)
                chunk(FC - 2, PAIRS - 1, 0)
                chunk(FC - 1, PAIRS - 1, 1, last=True)
                for c in range(DC):
                    if out is None:
                        squares.scalar(act_, c, y_added, DC * (PAIRS - 1) + c + 1)
                    else:
                        act_.wait_ge(out_turned, c + 1)
                        if c >= 2:
                            act_.wait_ge(core.stored[c % 2], 16 * (c // 2))
                        act_.activation(y_nat[:, c % 2], out_psum[c % 2][:, :].rearrange("p (b n) -> p b n", b=SB),
                                        ACT.Copy).then_inc(out_copied, 1)

            @block.gpsimd
            def _(pool):
                norm.gpsimd(pool)
                if out is None:
                    squares.gpsimd(pool)

            @block.vector
            def _(dve):
                def split_lo(n, k):
                    dve.wait_ge(hi_done[n], k + 1)
                    dve.tensor_tensor(lo[n][:, :, :], raw[n][:, :, :], hi[n][:, :, :].bitcast(F32), ALU.subtract)\
                       .then_inc(lo_done[n], 1)

                def taps(n, k):
                    dve.wait_ge(tap2[n], k + 1)
                    dve.scalar_tensor_tensor(acc[n][:, 1:S], pre[n][:, 0:S - 1], tap(n, 1, k), acc[n][:, 1:S],
                                             ALU.mult, ALU.add).then_inc(tap1[n], 1)
                    dve.wait_ge(tap1[n], k + 1)
                    dve.scalar_tensor_tensor(acc[n][:, 2:S], pre[n][:, 0:S - 2], tap(n, 0, k), acc[n][:, 2:S],
                                             ALU.mult, ALU.add).then_inc(conv[n], 1)

                def add_down(i, behind=lambda c: None):
                    for c in range(DC):
                        dve.wait_ge(y_ready, DC * i + c + 1)
                        dve.tensor_tensor(core.xT[:, c, :], y_psum[c % 2][:, :], core.xT[:, c, :], ALU.add)\
                           .then_inc(y_added, 1)
                        behind(c)

                def chunk(k, i, slot, last=False, first_pair=False, first=False):
                    taps("gate", k)
                    if slot == 0 and not first_pair:
                        add_down(i - 1, lambda c: split_lo("gate", k + 1) if c == 1 else None)
                    elif not last:
                        split_lo("gate", k + 1)
                    if slot == 0:
                        split_lo("down", i)
                    taps("up", k)
                    dve.wait_ge(conv["up"], k + 1)
                    dve.wait_ge(gated, k + 1)
                    if not first:
                        dve.wait_ge(act_lo_done, k)
                    dve.tensor_tensor(act, silu, up_acc, ALU.mult).then_inc(multiplied, 1)
                    if not last:
                        split_lo("up", k + 1)
                    dve.wait_ge(act_hi_done, k + 1)
                    dve.tensor_tensor(act_lo[:, slot, :], act, act_hi[:, slot, :].bitcast(F32), ALU.subtract)\
                       .then_inc(act_lo_done, 1)

                norm.vector(dve, lambda n: split_lo("gate", 0) if n == -1 else split_lo("up", 0) if n == 3 else None)
                chunk(0, 0, 0, first_pair=True, first=True)
                chunk(1, 0, 1)
                with dve.Fori(1, PAIRS - 1) as i:
                    chunk(2 * i, i, 0)
                    chunk(2 * i + 1, i, 1)
                chunk(FC - 2, PAIRS - 1, 0)
                chunk(FC - 1, PAIRS - 1, 1, last=True)
                if out is None:
                    add_down(PAIRS - 1, lambda c: squares.vector(dve, c - 1) if c else None)
                    squares.vector(dve, DC - 1)
                    squares.average(dve)
                else:
                    add_down(PAIRS - 1)


HD = 64
BIG = 1e30
GROUP = 512
TOPK = 256


def shape_constants():
    f = np.float32
    out = {"ident": np.eye(P, dtype=f)}
    pos = np.arange(S, dtype=f)[:, None]
    for dim in (64, 32):
        half = dim // 2
        inv = np.power(f(10000.0), -np.arange(half, dtype=f) / f(half)).astype(f)
        angle = (pos * inv[None, :]).astype(f)
        cos, sin = np.cos(angle).astype(f), np.sin(angle).astype(f)
        out[f"cos{dim}"] = np.concatenate([cos, cos], 1).reshape(SB, P, dim).transpose(1, 0, 2).copy()
        out[f"sin{dim}"] = np.concatenate([-sin, sin], 1).reshape(SB, P, dim).transpose(1, 0, 2).copy()
    chunk = 64
    q_chunk = 2 + np.arange(P)[:, None] // chunk
    k_chunk = np.arange(2 * P)[None, :] // chunk
    seen = (k_chunk <= q_chunk) & (k_chunk >= q_chunk - 1)
    out["window_mask"] = np.where(seen, f(0), f(BIG)).astype(f)
    return out


def heads_of(ap, width=HD):
    return ap.rearrange("p (h w) -> p h w", w=width)


def spread(ap, heads):
    return ap.unsqueeze(1).broadcast_to([P, heads, ap.shape[1]])


def each(ap, width):
    return ap.unsqueeze(2).broadcast_to([P, ap.shape[1], width])


class InProjection:

    AHEAD = 4

    def __init__(self, ph, norm, groups, w, banks, wide=GROUP):
        self.norm, self.groups, self.w, self.banks = norm, groups, w, banks
        self.raw = ph.sbuf("w_raw", [P, self.AHEAD, wide])
        self.hi = ph.sbuf("w_hi", [P, DC, wide], F32R)
        self.lo = ph.sbuf("w_lo", [P, DC, wide], F32R)
        self.loaded = [ph.sem(f"w_loaded{i}") for i in range(self.AHEAD)]
        self.hi_done, self.lo_done, self.used = ph.sem("w_hi_done"), ph.sem("w_lo_done"), ph.sem("w_used")
        self.ready = ph.sem("tile_ready")

    def width(self, g):
        return sum(n for _, n in self.groups[g])

    def bank(self, tile):
        return self.banks[tile % len(self.banks)]

    def sync(self, sp):
        for g, parts in enumerate(self.groups):
            for c in range(DC):
                u = DC * g + c
                if u >= self.AHEAD:
                    sp.wait_ge(self.lo_done, u - self.AHEAD + 1)
                at = 0
                for start, n in parts:
                    sp.dma_start(self.raw[:, u % self.AHEAD, at:at + n], self.w[c * P:(c + 1) * P, start:start + n])\
                      .then_inc(self.loaded[u % self.AHEAD], 16)
                    at += n

    def loads(self, u):
        return sum(len(self.groups[v // DC]) for v in range(u % self.AHEAD, u + 1, self.AHEAD))

    def split_hi(self, act, g, c):
        n, u = self.width(g), DC * g + c
        act.wait_ge(self.loaded[u % self.AHEAD], 16 * self.loads(u))
        if g and c < DC - 1:
            act.wait_ge(self.used, (DC - 1) * (g - 1) + c + 1)
        elif g:
            act.wait_ge(self.ready, SB * g)
        act.activation(self.hi[:, c, 0:n], self.raw[:, u % self.AHEAD, 0:n], ACT.Copy).then_inc(self.hi_done, 1)

    def split_lo(self, pool, g, c):
        n, u = self.width(g), DC * g + c
        pool.wait_ge(self.hi_done, u + 1)
        pool.tensor_tensor(self.lo[:, c, 0:n], self.raw[:, u % self.AHEAD, 0:n], self.hi[:, c, 0:n].bitcast(F32),
                           ALU.subtract).then_inc(self.lo_done, 1)

    def ends_group(self, tile):
        return tile % SB == SB - 2 and tile // SB + 1 < len(self.groups)

    def tensor(self, pe, tile, behind=lambda c: None):
        g, b = tile // SB, tile % SB
        n, norm = self.width(g), self.norm
        for c in range(DC):
            if b == 0:
                pe.wait_ge(self.lo_done, DC * g + c + 1)
            if g == 0 and b % (SB // 2) == 0:
                norm.wait_lo(pe, b // (SB // 2) * DC + c)
            for i in range(2):
                t = slice((b + i) * P, (b + i + 1) * P)
                ins = split_matmuls(pe, self.bank(tile + i)[:, 0:n], norm.hi[:, c, t], norm.lo[:, c, t],
                                    self.hi[:, c, 0:n], self.lo[:, c, 0:n], c == 0, c == DC - 1)
                if c == DC - 1:
                    ins.then_inc(self.ready, 1)
            if b == SB - 2 and c < DC - 1:
                ins.then_inc(self.used, 1)
            behind(c)


class Item:

    def __init__(self, src, dst, gain, mean_scale=1.0 / HD, mean_add=EPS, turn=None, cos=None, sin=None, shared=None):
        self.src, self.dst, self.gain = src, dst, gain
        self.heads, self.width = dst.shape[1], dst.shape[2]
        self.mean_scale, self.mean_add = mean_scale, mean_add
        self.turn, self.cos, self.sin, self.shared = turn, cos, sin, shared
        self.after = None


class Heads:

    ROOTS = 8

    def __init__(self, core, ph, tiles, copies, ready, most=8 * HD, most_turned=8 * HD):
        self.core, self.tiles, self.copies, self.ready = core, tiles, copies, ready
        self.sq = [ph.sbuf(f"sq{i}", [P, most]) for i in range(2)]
        self.part_cos = [ph.sbuf(f"part_cos{i}", [P, most_turned]) for i in range(2)]
        self.part_sin = [ph.sbuf(f"part_sin{i}", [P, most_turned]) for i in range(2)]
        self.mean = ph.sbuf("head_mean", [P, self.ROOTS, 8])
        self.total = ph.sbuf("head_total", [P, self.ROOTS, 8])
        self.rstd = ph.sbuf("head_rstd", [P, self.ROOTS, 8])
        self.squared, self.copied, self.placed = ph.sem("squared_heads"), ph.sem("copied"), ph.sem("placed")
        self.totalled, self.averaged, self.rooted = ph.sem("totalled"), ph.sem("averaged"), ph.sem("rooted_heads")
        self.scaled, self.cos_done, self.sin_done = ph.sem("scaled_heads"), ph.sem("cos_done"), ph.sem("sin_done")
        self.finished = ph.sem("finished")
        self.first, self.normed, self.copied_by = [0], [0], [0]
        turned = []
        for items, parts in zip(tiles, copies):
            for i, item in enumerate(items):
                item.index = self.first[-1] + i
                item.norm_index = self.normed[-1] + len([x for x in items[:i] if x.gain is not None])
                item.turn_index = len(turned)
                item.turned_before = turned[-2] if len(turned) >= 2 else None
                if item.turn is not None:
                    turned.append(item.index)
            self.first.append(self.first[-1] + len(items))
            self.normed.append(self.normed[-1] + len([x for x in items if x.gain is not None]))
            self.copied_by.append(self.copied_by[-1] + len(parts))

    def wait_scalar(self, eng, tile):
        if self.normed[tile + 1]:
            eng.wait_ge(self.squared, self.normed[tile + 1])
        if self.copied_by[tile + 1]:
            eng.wait_ge(self.copied, self.copied_by[tile + 1])

    def wait_taken(self, pe, tile):
        if self.first[tile + 1]:
            pe.wait_ge(self.placed, self.first[tile + 1])
        self.wait_scalar(pe, tile)

    def scalar(self, act, tile):
        if self.copies[tile] or any(item.gain is not None for item in self.tiles[tile]):
            act.wait_ge(self.ready, tile + 1)
        for item in self.tiles[tile]:
            if item.gain is None:
                continue
            k, n = item.norm_index, item.heads * item.width
            if k >= 2:
                act.wait_ge(self.totalled, k - 1)
            act.activation(heads_of(self.sq[k % 2][:, 0:n], item.width), item.src, ACT.Square).then_inc(self.squared, 1)
        for src, dst, scale in self.copies[tile]:
            act.activation(dst, src, ACT.Copy, scale=scale).then_inc(self.copied, 1)

    def place(self, dve, tile):
        if self.tiles[tile]:
            dve.wait_ge(self.ready, tile + 1)
            self.wait_scalar(dve, tile)
        for item in self.tiles[tile]:
            if item.after is not None and item.after[1] > 0:
                dve.wait_ge(*item.after)
            if item.gain is None:
                dve.tensor_copy(item.dst, item.src).then_inc(self.placed, 1)
                continue
            dve.tensor_tensor(item.dst, item.src, spread(item.gain, item.heads), ALU.mult).then_inc(self.placed, 1)
            k, n = item.norm_index, item.heads * item.width
            dve.tensor_reduce(self.total[:, k % self.ROOTS, 0:item.heads], heads_of(self.sq[k % 2][:, 0:n], item.width),
                              AX.X, ALU.add).then_inc(self.totalled, 1)
        for item in self.tiles[tile]:
            if item.gain is None:
                continue
            k = item.norm_index
            dve.wait_ge(self.totalled, k + 1)
            dve.tensor_scalar(self.mean[:, k % self.ROOTS, 0:item.heads], self.total[:, k % self.ROOTS, 0:item.heads],
                              item.mean_scale, item.mean_add, ALU.mult, ALU.add).then_inc(self.averaged, 1)

    def root(self, pool, tile):
        for item in self.tiles[tile]:
            if item.gain is None:
                continue
            k = item.norm_index
            pool.wait_ge(self.averaged, k + 1)
            pool.tensor_tensor(self.rstd[:, k % self.ROOTS, 0:item.heads], self.mean[:, k % self.ROOTS, 0:item.heads],
                               self.core.minus_half[:, 0:item.heads], ALU.pow).then_inc(self.rooted, 1)

    def sine(self, pool, tile):
        for item in self.tiles[tile]:
            if item.turn is None:
                continue
            width = item.turn.shape[2]
            j, n, half = item.turn_index, item.heads * width, width // 2
            if item.gain is None:
                pool.wait_ge(self.placed, item.index + 1)
            else:
                pool.wait_ge(self.scaled, item.norm_index + 1)
            if item.turned_before is not None:
                pool.wait_ge(self.finished, item.turned_before + 1)
            out = heads_of(self.part_sin[j % 2][:, 0:n], width)
            pool.tensor_tensor(out[:, :, 0:half], item.turn[:, :, half:width], spread(item.sin[:, 0:half], item.heads),
                               ALU.mult)
            pool.tensor_tensor(out[:, :, half:width], item.turn[:, :, 0:half],
                               spread(item.sin[:, half:width], item.heads), ALU.mult).then_inc(self.sin_done, 1)

    def gpsimd(self, pool, tile):
        if tile < len(self.tiles):
            self.root(pool, tile)
        if tile:
            self.sine(pool, tile - 1)

    def vector(self, dve, tile):
        if tile < len(self.tiles):
            self.place(dve, tile)
        if tile >= 2:
            self.finish(dve, tile - 2)
        if 1 <= tile <= len(self.tiles):
            self.scale(dve, tile - 1)

    def scale(self, dve, tile):
        for item in self.tiles[tile]:
            k = item.norm_index
            if item.gain is not None:
                dve.wait_ge(self.placed, item.index + 1)
                dve.wait_ge(self.rooted, k + 1)
                dve.tensor_tensor(item.dst, item.dst, each(self.rstd[:, k % self.ROOTS, 0:item.heads], item.width), ALU.mult)\
                   .then_inc(self.scaled, 1)
        for item in self.tiles[tile]:
            j = item.turn_index
            if item.turn is not None:
                width = item.turn.shape[2]
                if item.gain is not None:
                    dve.wait_ge(self.scaled, item.norm_index + 1)
                else:
                    dve.wait_ge(self.placed, item.index + 1)
                dve.tensor_tensor(heads_of(self.part_cos[j % 2][:, 0:item.heads * width], width), item.turn,
                                  spread(item.cos, item.heads), ALU.mult).then_inc(self.cos_done, 1)

    def finish(self, dve, tile):
        for item in self.tiles[tile]:
            j, k = item.turn_index, item.norm_index
            if item.turn is not None:
                width = item.turn.shape[2]
                n = item.heads * width
                dve.wait_ge(self.cos_done, j + 1)
                dve.wait_ge(self.sin_done, j + 1)
                dve.tensor_tensor(item.turn, heads_of(self.part_cos[j % 2][:, 0:n], width),
                                  heads_of(self.part_sin[j % 2][:, 0:n], width), ALU.add).then_inc(self.finished, 1)
            else:
                dst, src = item.shared
                dve.wait_ge(self.scaled, k + 1)
                dve.tensor_tensor(dst, spread(src, item.heads), each(self.rstd[:, k % self.ROOTS, 0:item.heads], src.shape[1]),
                                  ALU.mult).then_inc(self.finished, 1)


class Unit:

    def __init__(self, products, v, mask=None, start=None):
        self.products, self.v, self.mask, self.start = products, v, mask, start
        self.n = products[0][1].shape[1]


class Stack:

    def __init__(self, core, ph, heads, bank):
        self.core, self.heads, self.bank = core, heads, bank
        self.pair = ph.sbuf("q_pair", [P, heads, 2, HD], F32R)
        self.stack = ph.product_sbuf("q_stack", [P, 2, heads, P])
        self.hi_done, self.lo_done = ph.sem("q_hi_done"), ph.sem("q_lo_done")
        self.turned, self.copied = ph.sem("q_turned"), ph.sem("q_copied")

    def split_hi(self, act, j, q):
        if j:
            act.wait_ge(self.turned, j)
        act.activation(self.pair[:, :, 0, :], q, ACT.Copy).then_inc(self.hi_done, 1)

    def split_lo(self, pool, j, q):
        pool.wait_ge(self.hi_done, j + 1)
        if j:
            pool.wait_ge(self.turned, j)
        pool.tensor_tensor(self.pair[:, :, 1, :], q, self.pair[:, :, 0, :].bitcast(F32), ALU.subtract)\
            .then_inc(self.lo_done, 1)

    def turn(self, pe, j):
        pe.wait_ge(self.lo_done, j + 1)
        if j:
            pe.wait_ge(self.copied, j)
        for i in range(self.heads):
            ins = pe.transpose(self.bank[:, i * P:(i + 1) * P],
                               self.pair[:, i].rearrange("p a w -> p (a w)").bitcast(F32), self.core.ident[:, :])
        ins.then_inc(self.turned, 1)

    def source(self):
        return self.bank[:, 0:self.heads * P].rearrange("p (c s) -> p c s", c=self.heads)


class Attention:

    def __init__(self, core, ph, rows, outs, sinks=None, most=S, copy_on_vector=lambda u: False,
                 turned=None, depth=2):
        self.core, self.outs, self.sinks = core, outs, sinks
        self.units = [u for row in rows for u in row]
        self.R = len(rows[0])
        self.depth, self.turn_lag, self.weight_lag = depth, depth - 1, depth
        self.on_vector = [copy_on_vector(u) for u in range(len(self.units))]
        self.scores = [ph.psum(f"scores{i}", max(most, GROUP)) for i in range(depth)]
        self.turned = [ph.psum("turned", max(most, GROUP))] if turned is None else turned
        self.out = [ph.psum(f"out{i}", GROUP) for i in range(2)]
        self.p = [ph.sbuf(f"p{i}", [P, most]) for i in range(depth)]
        self.pt = [ph.sbuf(f"pt{i}", [P, most]) for i in range(2)]
        self.low = ph.sbuf("low", [P, 2, self.R])
        self.sum = ph.sbuf("sum", [P, 2, self.R])
        self.inverse = ph.sbuf("inverse", [P, 2, self.R])
        self.sink = ph.sbuf("sink_part", [P, 2, self.R])
        self.scored, self.cornered = ph.sem("scored"), ph.sem("cornered")
        self.lowest, self.exped = ph.sem("lowest"), ph.sem("exped")
        self.turns, self.by_scalar, self.by_vector = ph.sem("turns"), ph.sem("copied_by_scalar"), ph.sem("copied_by_vector")
        self.weighted, self.divided, self.inverted = ph.sem("weighted"), ph.sem("divided"), ph.sem("inverted")
        self.sink_shifted, self.sink_exped = ph.sem("sink_shifted"), ph.sem("sink_exped")
        self.sink_added = ph.sem("sink_added")

    def wait_copied(self, eng, u):
        n = len([i for i in range(u + 1) if self.on_vector[i] == self.on_vector[u]])
        eng.wait_ge(self.by_vector if self.on_vector[u] else self.by_scalar, n)

    def score(self, pe, u):
        unit = self.units[u]
        if u >= self.depth:
            pe.wait_ge(self.exped, u - self.depth + 1)
        last = len(unit.products) - 1
        for at in range(0, unit.n, GROUP):
            n = min(GROUP, unit.n - at)
            for i, (q, k) in enumerate(unit.products):
                ins = pe.matmul(self.scores[u % self.depth][:, at:at + n], q, k[:, at:at + n], start=i == 0, stop=i == last)
        ins.then_inc(self.scored, 1)

    def turn(self, pe, u):
        unit = self.units[u]
        pe.wait_ge(self.exped, u + 1)
        banks = len(self.turned)
        for v in range(max(0, u - banks), u - banks + 1):
            self.wait_copied(pe, v)
        for at in range(0, unit.n, P):
            ins = pe.transpose(self.turned[u % banks][:, at:at + P], self.p[u % self.depth][:, at:at + P], self.core.ident[:, :])
        ins.then_inc(self.turns, 1)

    def weight(self, pe, u):
        unit, row, h = self.units[u], u // self.R, u % self.R
        self.wait_copied(pe, u)
        if h == 0 and row >= 2:
            pe.wait_ge(self.divided, row - 1)
        for i, v in enumerate(unit.v):
            ins = pe.matmul(self.out[row % 2][:, h * HD:(h + 1) * HD], self.pt[u % 2][:, i * P:(i + 1) * P], v,
                            start=i == 0, stop=i == len(unit.v) - 1)
        ins.then_inc(self.weighted, 1)

    def tensor(self, pe, before=lambda u: None, after_score=lambda u: None):
        n = len(self.units)
        for u in range(n + self.weight_lag):
            before(u)
            if u < n:
                self.score(pe, u)
            after_score(u)
            if 0 <= u - self.turn_lag < n:
                self.turn(pe, u - self.turn_lag)
            if u >= self.weight_lag:
                self.weight(pe, u - self.weight_lag)

    def lowest_of(self, dve, u):
        unit, row, h = self.units[u], u // self.R, u % self.R
        dve.wait_ge(self.scored, u + 1)
        if h == 0 and row >= 2:
            dve.wait_ge(self.exped, self.R * (row - 1))
        s = self.scores[u % self.depth][:, 0:unit.n]
        low = self.low[:, row % 2, h:h + 1]
        if unit.mask is not None:
            if u >= self.depth:
                dve.wait_ge(self.turns, u - self.depth + 1)
            dve.tensor_tensor_reduce(self.p[u % self.depth][:, 0:unit.n], s, unit.mask, 1.0,
                                     BIG if unit.start is None else unit.start, ALU.add, ALU.min, low)\
               .then_inc(self.lowest, 1)
            return
        dve.memset(self.scores[u % self.depth][0:P // 2, unit.n - P // 2:unit.n], BIG).then_inc(self.cornered, 1)
        dve.wait_ge(self.cornered, len([x for x in self.units[:u + 1] if x.mask is None]))
        dve.tensor_reduce(low, s, AX.X, ALU.min).then_inc(self.lowest, 1)

    def exps(self, act, u):
        unit, row, h = self.units[u], u // self.R, u % self.R
        act.wait_ge(self.lowest, u + 1)
        if u >= self.depth:
            act.wait_ge(self.turns, u - self.depth + 1)
        if h == 0 and row >= 2:
            act.wait_ge(self.divided, row - 1)
        s = self.p[u % self.depth] if unit.mask is not None else self.scores[u % self.depth]
        act.activation(self.p[u % self.depth][:, 0:unit.n], s[:, 0:unit.n], ACT.Exp, bias=self.low[:, row % 2, h:h + 1],
                       scale=-1.0, accum_out=self.sum[:, row % 2, h:h + 1]).then_inc(self.exped, 1)

    def copy(self, eng, u, vector):
        if self.on_vector[u] != vector:
            return
        unit = self.units[u]
        eng.wait_ge(self.turns, u + 1)
        if u >= 2:
            eng.wait_ge(self.weighted, u - 1)
        dst, src = self.pt[u % 2][:, 0:unit.n], self.turned[u % len(self.turned)][:, 0:unit.n]
        if vector:
            eng.tensor_copy(dst, src).then_inc(self.by_vector, 1)
        else:
            eng.activation(dst, src, ACT.Copy).then_inc(self.by_scalar, 1)

    def scalar(self, act, between=lambda u: None):
        n = len(self.units)
        for u in range(n + self.turn_lag):
            between(u)
            if u >= self.turn_lag:
                self.copy(act, u - self.turn_lag, False)
            if u < n:
                self.exps(act, u)
            if u < n and self.sinks is not None and (u + 1) % self.R == 0:
                row = u // self.R
                act.wait_ge(self.sink_shifted, row + 1)
                act.activation(self.sink[:, row % 2, :], self.sink[:, row % 2, :], ACT.Exp).then_inc(self.sink_exped, 1)

    def divide(self, dve, row):
        dve.wait_ge(self.exped, self.R * (row + 1))
        total = self.sum[:, row % 2, :]
        if self.sinks is not None:
            dve.wait_ge(self.sink_exped, row + 1)
            dve.tensor_tensor(total, total, self.sink[:, row % 2, :], ALU.add).then_inc(self.sink_added, 1)
            dve.wait_ge(self.sink_added, row + 1)
        dve.reciprocal(self.inverse[:, row % 2, :], total).then_inc(self.inverted, 1)
        dve.wait_ge(self.inverted, row + 1)
        dve.wait_ge(self.weighted, self.R * (row + 1))
        dve.tensor_tensor(self.outs[row], heads_of(self.out[row % 2][:, 0:self.R * HD]),
                          each(self.inverse[:, row % 2, :], HD), ALU.mult).then_inc(self.divided, 1)

    def vector(self, dve, between=lambda u: None, behind=lambda u: None):
        n = len(self.units)
        for u in range(n + self.weight_lag + 1):
            if u < n:
                self.lowest_of(dve, u)
                if self.sinks is not None and (u + 1) % self.R == 0:
                    row = u // self.R
                    dve.wait_ge(self.lowest, u + 1)
                    if row >= 2:
                        dve.wait_ge(self.sink_added, row - 1)
                    dve.tensor_tensor(self.sink[:, row % 2, :], self.low[:, row % 2, :], self.sinks[row], ALU.add)\
                       .then_inc(self.sink_shifted, 1)
            between(u)
            if 0 <= u - self.turn_lag < n:
                self.copy(dve, u - self.turn_lag, True)
            if u > self.weight_lag and (u - self.weight_lag) % self.R == 0:
                self.divide(dve, (u - self.weight_lag) // self.R - 1)
            behind(u)


def out_projection(core, tag, mixed, w):
    nc = core.nc
    with Phase(nc, tag) as ph:
        hi, lo = ph.sbuf("mix_hi", [P, DC, S], F32R), ph.sbuf("mix_lo", [P, DC, S], F32R)
        raw = ph.sbuf("raw", [P, 2, DC, P])
        w_hi, w_lo = ph.sbuf("w_hi", [P, 2, DC, P], F32R), ph.sbuf("w_lo", [P, 2, DC, P], F32R)
        turned = [ph.psum(f"turned{i}", GROUP) for i in range(4)]
        y = [ph.psum(f"y{i}", S) for i in range(2)]
        turns, hi_done, lo_done = ph.sem("turns"), ph.sem("hi_done"), ph.sem("lo_done")
        squares = SquareSum(core, ph, turned[0], ph.sbuf("square", [P, 2, S]), ph.sbuf("square_total", [P, S])[:, :])
        loaded = [ph.sem(f"loaded{i}") for i in range(2)]
        w_hi_done, w_lo_done, product, added = ph.sem("w_hi_done"), ph.sem("w_lo_done"), ph.sem("product"), ph.sem("added")
        view = w.rearrange("(c p) n -> p c n", p=P)
        TURNS = 2 * SB

        def place(t):
            b, c = t // 2, 4 * (t % 2)
            return slice(c, c + 4), slice(b * P, (b + 1) * P)

        with nc.Block() as block:
            @block.sync
            def _(sp):
                for c in range(DC):
                    if c >= 2:
                        sp.wait_ge(w_lo_done, c - 1)
                    sp.dma_start(raw[:, c % 2], view[:, :, c * P:(c + 1) * P]).then_inc(loaded[c % 2], 16)

            @block.scalar
            def _(act):
                def weights(c):
                    act.wait_ge(loaded[c % 2], 16 * (c // 2 + 1))
                    if c >= 2:
                        act.wait_ge(product, c - 1)
                    act.activation(w_hi[:, c % 2], raw[:, c % 2], ACT.Copy).then_inc(w_hi_done, 1)

                for t in range(TURNS):
                    act.wait_ge(turns, t + 1)
                    f, s = place(t)
                    act.activation(hi[:, f, s], turned[t % 4].rearrange("p (c s) -> p c s", c=4), ACT.Copy)\
                       .then_inc(hi_done, 1)
                    if t in (3, 7):
                        weights(t // 4)
                for c in range(2, DC + 2):
                    if c < DC:
                        weights(c)
                    squares.scalar(act, c - 2, added, c - 1)

            @block.gpsimd
            def _(pool):
                for c in range(DC):
                    pool.wait_ge(w_hi_done, c + 1)
                    pool.tensor_tensor(w_lo[:, c % 2], raw[:, c % 2], w_hi[:, c % 2].bitcast(F32), ALU.subtract)\
                        .then_inc(w_lo_done, 1)
                squares.gpsimd(pool)

            @block.vector
            def _(dve):
                for t in range(TURNS):
                    dve.wait_ge(hi_done, t + 1)
                    f, s = place(t)
                    dve.tensor_tensor(lo[:, f, s], turned[t % 4].rearrange("p (c s) -> p c s", c=4),
                                      hi[:, f, s].bitcast(F32), ALU.subtract).then_inc(lo_done, 1)
                for c in range(DC):
                    dve.wait_ge(product, c + 1)
                    dve.tensor_tensor(core.xT[:, c, :], y[c % 2][:, :], core.xT[:, c, :], ALU.add).then_inc(added, 1)
                    if c:
                        squares.vector(dve, c - 1)
                squares.vector(dve, DC - 1)
                squares.average(dve)

            @block.tensor
            def _(pe):
                for t in range(TURNS):
                    f, s = place(t)
                    if t >= 4:
                        pe.wait_ge(lo_done, t - 3)
                    for i in range(4):
                        c = 4 * (t % 2) + i
                        ins = pe.transpose(turned[t % 4][:, i * P:(i + 1) * P], mixed(t // 2, c), core.ident[:, :])
                    ins.then_inc(turns, 1)
                for c in range(DC):
                    pe.wait_ge(w_lo_done, c + 1)
                    if c >= 2:
                        pe.wait_ge(added, c - 1)
                    for h in range(2):
                        t = slice(h * GROUP, (h + 1) * GROUP)
                        if c == 0:
                            pe.wait_ge(lo_done, SB * (h + 1))
                        for f in range(DC):
                            ins = split_matmuls(pe, y[c % 2][:, t], w_hi[:, c % 2, f], w_lo[:, c % 2, f],
                                                hi[:, f, t], lo[:, f, t], f == 0, f == DC - 1)
                    ins.then_inc(product, 1)
                squares.tensor(pe)


def window_mixer(core, t):
    nc = core.nc
    QH, KH, KV = 16, 2, 2 * HD
    with Phase(nc, "window") as outer:
        k_nat = outer.sbuf("k", [P, SB, KV])
        v_nat = outer.sbuf("v", [P, SB, KV])
        q_nat = outer.sbuf("q", [P, SB, QH * HD])
        kT = outer.sbuf("kT", [P, KH, 2, S], F32R)
        small = outer.sbuf("small", [P, 2 * HD + QH])
        gain_q, gain_k, sinks = small[:, 0:HD], small[:, HD:2 * HD], small[:, 2 * HD:]
        row = outer.sbuf("row", [1, 2 * HD + QH])
        cos, sin, mask = outer.sbuf("cos", [P, SB, HD]), outer.sbuf("sin", [P, SB, HD]), outer.sbuf("mask", [P, 2 * P])

        with Phase(nc, "window_in") as ph:
            banks = [ph.psum(f"tile{i}", GROUP) for i in range(4)]
            rstd_psum = ph.psum("rstd", S)
            turned = rstd_psum
            sum_psum = ph.psum("sum", GROUP)
            norm = Norm(core, ph, COL_O_NORM, rstd_psum)
            norm.buffers(q_nat.rearrange("p b n -> p (b n)")[:, 0:3 * S])
            W = 6 * HD
            groups = [[(QH * HD, 2 * KV)]] + [[(at, min(W, QH * HD - at))] for at in range(0, QH * HD, W)]
            proj = InProjection(ph, norm, groups, t["o_w_in"][0], banks, W)
            tiles, copies = [], []
            for g in range(len(groups)):
                for b in range(SB):
                    bank = proj.bank(SB * g + b)
                    if g == 0:
                        k = heads_of(k_nat[:, b, :])
                        tiles.append([Item(heads_of(bank[:, 0:KV]), k, gain_k, turn=k, cos=cos[:, b, :], sin=sin[:, b, :])])
                        copies.append([(bank[:, KV:2 * KV], v_nat[:, b, :], 1.0)])
                    else:
                        start, n = groups[g][0]
                        q = heads_of(q_nat[:, b, start:start + n])
                        tiles.append([Item(heads_of(bank[:, 0:n]), q, gain_q, 1.0, HD * EPS, q, cos[:, b, :], sin[:, b, :])])
                        copies.append([])
            heads = Heads(core, ph, tiles, copies, proj.ready, W, W)
            consts, rows, spread_done, small_done = ph.sem("consts"), ph.sem("rows"), ph.sem("gains_spread"), ph.sem("small_done")
            k_turns, k_copied = ph.sem("k_turns"), ph.sem("k_copied")
            k_twice = ph.sbuf("k_twice", [P, KH, 2, 2, HD], F32R)
            k_hi_done, k_doubled = ph.sem("k_hi_done"), ph.sem("k_doubled")
            T = SB * len(groups)
            with nc.Block() as block:
                @block.sync
                def _(sp):
                    sp.dma_start(row[:, 0:HD], t["o_qnorm"]).then_inc(rows, 16)
                    sp.dma_start(row[:, HD:2 * HD], t["o_knorm"]).then_inc(rows, 16)
                    sp.dma_start(row[:, 2 * HD:], t["o_sinks"]).then_inc(rows, 16)
                    sp.dma_start(cos[:, :, :], t["cos64"]).then_inc(consts, 16)
                    sp.dma_start(sin[:, :, :], t["sin64"]).then_inc(consts, 16)
                    sp.dma_start(mask[:, :], t["window_mask"]).then_inc(consts, 16)
                    proj.sync(sp)

                def turned_k(act, b):
                    act.wait_ge(k_turns, b + 1)
                    act.activation(kT[:, :, :, b * P:(b + 1) * P].rearrange("p h a s -> p (h a) s"),
                                   turned[:, (b % 2) * GROUP:(b % 2 + 1) * GROUP].rearrange("p (h s) -> p h s", h=2 * KH),
                                   ACT.Copy).then_inc(k_copied, 1)

                @block.scalar
                def _(act):
                    proj.split_hi(act, 0, 0)
                    proj.split_hi(act, 0, 1)
                    norm.scalar(act, lambda n: proj.split_hi(act, 0, n // 2 + 2) if n % 2 and n // 2 + 2 < DC else None)
                    for pair in range(0, T, 2):
                        for tile in (pair, pair + 1):
                            heads.scalar(act, tile)
                            if 4 <= tile < SB + 4:
                                turned_k(act, tile - 4)
                        if proj.ends_group(pair + 2):
                            for c in range(DC):
                                proj.split_hi(act, (pair + 2) // SB + 1, c)

                @block.gpsimd
                def _(pool):
                    proj.split_lo(pool, 0, 0)
                    proj.split_lo(pool, 0, 1)
                    norm.gpsimd(pool, lambda n: proj.split_lo(pool, 0, n // 2 + 2) if n // 2 + 2 < DC else None)
                    pool.wait_ge(consts, 48)
                    for pair in range(0, T, 2):
                        for tile in (pair, pair + 1):
                            heads.gpsimd(pool, tile)
                        if proj.ends_group(pair + 2):
                            for c in range(DC):
                                proj.split_lo(pool, (pair + 2) // SB + 1, c)
                    heads.gpsimd(pool, T)

                @block.vector
                def _(dve):
                    norm.vector(dve)
                    norm.wait_lo(dve, norm.UNITS - 1)
                    dve.wait_ge(spread_done, 1)
                    dve.tensor_scalar(gain_q, sum_psum[:, P:P + HD], -1.0, None, ALU.mult)
                    dve.tensor_copy(small[:, HD:], sum_psum[:, P + HD:P + 2 * HD + QH]).then_inc(small_done, 1)
                    dve.wait_ge(small_done, 1)
                    dve.wait_ge(consts, 48)
                    for tile in range(T + 2):
                        heads.vector(dve, tile)
                        if 2 <= tile < SB + 2:
                            b = tile - 2
                            dve.wait_ge(heads.finished, b + 1)
                            if b >= 1:
                                dve.wait_ge(k_turns, b)
                            k = heads_of(k_nat[:, b, :]).unsqueeze(2).broadcast_to([P, KH, 2, HD])
                            dve.tensor_copy(k_twice[:, :, 0], k).then_inc(k_hi_done, 1)
                            dve.wait_ge(k_hi_done, b + 1)
                            dve.tensor_tensor(k_twice[:, :, 1], k, k_twice[:, :, 0].bitcast(F32), ALU.subtract)\
                               .then_inc(k_doubled, 1)

                @block.tensor
                def _(pe):
                    pe.wait_ge(rows, 48)
                    pe.matmul(sum_psum[:, P:P + 2 * HD + QH], core.ones[0:1, :], row[:, :], start=True, stop=True)\
                      .then_inc(spread_done, 1)
                    norm.tensor(pe)
                    for tile in range(T):
                        if tile % 2 == 0:
                            if tile >= len(banks):
                                heads.wait_taken(pe, tile + 1 - len(banks))
                            proj.tensor(pe, tile)
                        if 4 <= tile < SB + 4:
                            b = tile - 4
                            pe.wait_ge(k_doubled, b + 1)
                            if b >= 2:
                                pe.wait_ge(k_copied, b - 1)
                            for i in range(2 * KH):
                                at = (b % 2) * GROUP + i * P
                                ins = pe.transpose(turned[:, at:at + P],
                                                   k_twice[:, i // 2, i % 2].rearrange("p a w -> p (a w)").bitcast(F32),
                                                   core.ident[:, :])
                            ins.then_inc(k_turns, 1)

        with Phase(nc, "window_att") as ph:
            queries = Stack(core, ph, 4, ph.psum("q_bank", GROUP))
            neg = ph.sbuf("sinks_neg", [P, QH])
            rows, outs, sink_rows = [], [], []
            for b in range(SB):
                first = max(0, b - 1)
                for r in range(KH):
                    units = []
                    for i in range(8):
                        h = 8 * r + i
                        q = queries.stack[:, i // 4, i % 4, :]
                        units.append(Unit([(q, kT[:, r, part, first * P:(b + 1) * P]) for part in range(2)],
                                          [v_nat[:, c, r * HD:(r + 1) * HD] for c in range(first, b + 1)],
                                          mask=mask[:, (P if b == 0 else 0):], start=neg[:, h:h + 1]))
                    rows.append(units)
                    outs.append(heads_of(q_nat[:, b, r * GROUP:(r + 1) * GROUP]))
                    sink_rows.append(small[:, 2 * HD + 8 * r:2 * HD + 8 * r + 8])
            att = Attention(core, ph, rows, outs, sinks=sink_rows, most=2 * P,
                            depth=3,
                            turned=[ph.psum(f"turned{i}", GROUP) for i in range(2)])
            negated = ph.sem("negated")
            HALVES = 2 * len(rows)

            def q_half(j):
                return outs[j // 2][:, 4 * (j % 2):4 * (j % 2) + 4, :]

            with nc.Block() as block:
                @block.tensor
                def _(pe):
                    def before(u):
                        if u == 0:
                            queries.turn(pe, 0)
                        if u % 4 == 0 and u < len(att.units):
                            pe.wait_ge(queries.copied, u // 4 + 1)

                    def after_score(u):
                        if u % 4 == 2 and u // 4 + 1 < HALVES:
                            queries.turn(pe, u // 4 + 1)

                    att.tensor(pe, before, after_score)

                @block.gpsimd
                def _(pool):
                    for j in range(HALVES):
                        queries.split_lo(pool, j, q_half(j))

                @block.scalar
                def _(act):
                    queries.split_hi(act, 0, q_half(0))
                    att.scalar(act, lambda u: queries.split_hi(act, u // 4 + 1, q_half(u // 4 + 1))
                               if u % 4 == 0 and u // 4 + 1 < HALVES else None)

                @block.vector
                def _(dve):
                    def copy_queries(j):
                        dve.wait_ge(queries.turned, j + 1)
                        if j >= 2:
                            dve.wait_ge(att.scored, 4 * (j - 1))
                        dve.tensor_copy(queries.stack[:, j % 2], queries.source()).then_inc(queries.copied, 1)

                    dve.tensor_scalar(neg[:, :], small[:, 2 * HD:], -1.0, None, ALU.mult).then_inc(negated, 1)
                    dve.wait_ge(negated, 1)
                    copy_queries(0)
                    att.vector(dve, behind=lambda u: copy_queries(u // 4 + 1)
                               if u % 4 == 2 and u // 4 + 1 < HALVES else None)

        out_projection(core, "window_out", lambda b, c: q_nat[:, b, c * P:(c + 1) * P], t["o_w_out"][0])


class TopK:

    TAKEN, UNSEEN = -3e38, -2e38

    def __init__(self, ph, scores):
        self.scores, self.blocks = scores, sorted(scores)
        self.best = ph.sbuf("best", [P, 2, 8])
        self.unseen, self.found, self.taken = ph.sem("unseen"), ph.sem("found"), ph.sem("taken")
        self.per_pair = TOPK // 8
        self.rounds = self.per_pair * len(self.blocks) // 2
        self.done = 0

    def scored(self, dve, b, added, value):
        n = self.scores[b].shape[1]
        dve.wait_ge(added, value)
        dve.memset(self.scores[b][0:P // 2, n - P // 2:n], self.UNSEEN).then_inc(self.unseen, 1)

    def run(self, dve, until):
        steps = min(int(4 * until), 4 * self.rounds)
        while self.done < steps:
            r, replace, i = self.done // 4, self.done % 4 // 2, self.done % 2
            b = self.blocks[2 * (r // self.per_pair) + i]
            if not replace:
                if r % self.per_pair == 0:
                    dve.wait_ge(self.unseen, self.blocks.index(b) + 1)
                if r:
                    dve.wait_ge(self.taken, 2 * r - 1 + i)
                dve.max(self.best[:, i, :], self.scores[b]).then_inc(self.found, 1)
            else:
                dve.wait_ge(self.found, 2 * r + 1 + i)
                dve.match_replace(self.scores[b], self.best[:, i, :], self.scores[b], self.TAKEN)\
                   .then_inc(self.taken, 1)
            self.done += 1

    def spread_over(self, dve, units, start, end):
        total = sum(unit.n for unit in units)

        def hook(u, part=1.0):
            passed = sum(unit.n for unit in units[:u]) + (part * units[u].n if u < len(units) else 0)
            self.run(dve, start + (end - start) * min(1.0, passed / total))

        return hook

    def mask(self, dve, pair, done):
        dve.wait_ge(self.taken, 2 * self.per_pair * (pair + 1))
        for b in self.blocks[2 * pair:2 * pair + 2]:
            dve.tensor_scalar(self.scores[b], self.scores[b], self.TAKEN, BIG, ALU.not_equal, ALU.mult).then_inc(done, 1)


def global_mixer(core, t):
    nc = core.nc
    with Phase(nc, "global_mix") as mixes, ExitStack() as released:
        mix_a, bq = mixes.sbuf("mix_a", [P, SB, 8 * HD]), mixes.sbuf("bq", [P, SB, 8 * HD])
        outer = released.enter_context(Phase(nc, "global"))
        Q_LAT, KV_LAT, K_PE = 256, 128, 32
        LAT = Q_LAT + KV_LAT + K_PE
        seen = {b: (b + 1) * P for b in range(TOPK // P, SB)}
        behind = sum(seen.values()) - (SB * 8 - 4) * HD
        index_flat = outer.sbuf("index", [P, behind + SB * 8 * HD])
        iq = index_flat[:, behind:].rearrange("p (b n) -> p b n", b=SB)
        scores, at = {}, 0
        for b, n in seen.items():
            scores[b] = index_flat[:, at:at + n]
            at += n
        lat = outer.sbuf("lat", [P, SB, LAT])
        keys = outer.sbuf("keys", [P, SB, 2 * HD])
        bv = outer.sbuf("bv", [P, SB, HD])
        iw = outer.sbuf("iw", [P, SB, 8])
        keysT = outer.sbuf("keysT", [P, 2, S], F32R)
        parts = (("e_dsa_qnorm", HD), ("e_dsa_knorm", HD), ("e_idx_knorm", HD), ("e_mla_qnorm", 96),
                 ("e_mla_knorm", 96), ("e_qa_norm", Q_LAT), ("e_kva_norm", KV_LAT))
        n_gains = sum(n for _, n in parts)
        gains = outer.sbuf("gains", [P, n_gains])
        gain, at = {}, 0
        for name, n in parts:
            gain[name] = gains[:, at:at + n]
            at += n
        cos, sin = outer.sbuf("cos", [P, SB, HD]), outer.sbuf("sin", [P, SB, HD])
        lat_sum = outer.sbuf("lat_sum", [P, 3, SB])
        lat_rstd = outer.sbuf("lat_rstd", [P, 2, SB])
        turned_pe = outer.sbuf("turned_pe", [P, SB, K_PE])
        topk = TopK(outer, scores)
        CHOSEN = [30, 50, 64]
        index_phase(core, t, index_flat, iq, scores, seen, bq, lat, keys, bv, iw, keysT, parts, gains, gain, cos, sin,
                    lat_sum, mix_a, topk, CHOSEN[0])
        for group in range(2):
            with Phase(nc, f"latent{group}") as ph:
                qT, kT = ph.sbuf("qT", [P, 4, S]), ph.sbuf("kT", [P, 4, S])
                v = ph.sbuf("v", [P, SB, 4 * HD])
                latent_heads(core, t, group, lat, lat_sum, lat_rstd, turned_pe, gain, qT, kT, v)
                with Phase(nc, f"latent_att{group}") as inner:
                    rows = [[Unit([(qT[:, i, b * P:(b + 1) * P], kT[:, i, 0:(b + 1) * P])],
                                  [v[:, c, i * HD:(i + 1) * HD] for c in range(b + 1)]) for i in range(4)]
                            for b in range(SB)]
                    outs = [heads_of(mix_a[:, b, 4 * HD * group:4 * HD * (group + 1)]) for b in range(SB)]
                    att = Attention(core, inner, rows, outs)
                    with nc.Block() as block:
                        @block.tensor
                        def _(pe):
                            att.tensor(pe)

                        @block.scalar
                        def _(act):
                            att.scalar(act)

                        @block.vector
                        def _(dve):
                            choose = topk.spread_over(dve, att.units, CHOSEN[group], CHOSEN[group + 1])
                            att.vector(dve, lambda u: choose(u, 0.5), choose)
        topk_attention(core, topk, scores, bq, bv, keys)
        released.close()
        out_projection(core, "global_out", lambda b, c: (mix_a[:, b, c * P:(c + 1) * P] if c < 4 else
                                                         bq[:, b, (c - 4) * P:(c - 3) * P]), t["e_w_out"][0])


def index_phase(core, t, index_flat, iq, scores, seen, bq, lat, keys, bv, iw, keysT, parts, gains, gain, cos, sin,
                lat_sum, scratch, topk, rounds):
    nc = core.nc
    with Phase(nc, "index") as ph:
        banks = [ph.psum(f"tile{i}", GROUP) for i in range(4)]
        dots = [ph.psum(f"dots{i}", GROUP) for i in range(2)]
        rstd_psum = ph.psum("rstd", S)
        keys_bank, iq_bank = rstd_psum[:, 0:GROUP], rstd_psum[:, GROUP:S]
        norm = Norm(core, ph, COL_E_NORM, rstd_psum)
        norm.buffers(index_flat)
        IQ, BQ, BK, IK, IW = 1056, 416, 928, 1568, 1632
        W = 4 * HD
        groups = [[(IQ, W)], [(IQ + W, W)], [(BK, 2 * HD), (IK, HD + 8)], [(BQ, W)], [(BQ + W, W)], [(0, 208)], [(208, 208)]]
        proj = InProjection(ph, norm, groups, t["e_w_in"][0], banks, W)
        tiles, copies = [], []
        for g in range(len(groups)):
            for b in range(SB):
                bank = proj.bank(SB * g + b)
                turn = dict(cos=cos[:, b, :], sin=sin[:, b, :])
                if g < 2:
                    q = heads_of(iq[:, b, g * W:(g + 1) * W])
                    tiles.append([Item(heads_of(bank[:, 0:W]), q, None, turn=q, **turn)])
                    copies.append([])
                elif g == 2:
                    both = [heads_of(keys[:, b, i * HD:(i + 1) * HD]) for i in range(2)]
                    tiles.append([Item(heads_of(bank[:, 0:HD]), both[0], gain["e_dsa_knorm"], turn=both[0], **turn),
                                  Item(heads_of(bank[:, 2 * HD:3 * HD]), both[1], gain["e_idx_knorm"], turn=both[1], **turn)])
                    copies.append([(bank[:, HD:2 * HD], bv[:, b, :], 1.0),
                                   (bank[:, 3 * HD:3 * HD + 8], iw[:, b, :], (8 * HD) ** -0.5)])
                elif g < 5:
                    q = heads_of(bq[:, b, (g - 3) * W:(g - 2) * W])
                    tiles.append([Item(heads_of(bank[:, 0:W]), q, gain["e_dsa_qnorm"], 1.0, HD * EPS, q, **turn)])
                    copies.append([])
                else:
                    tiles.append([])
                    copies.append([(bank[:, 0:208], lat[:, b, (g - 5) * 208:(g - 4) * 208], 1.0)])
        ph.borrow(scratch.rearrange("p b n -> p (b n)"))
        heads = Heads(core, ph, tiles, copies, proj.ready, W, W)
        row = bq.rearrange("p b n -> p (b n)")[0:1, 0:gains.shape[1]]
        twice = ph.sbuf("twice", [P, 2, 2, 2 * HD], F32R).rearrange("p b a (t w) -> p b a t w", t=2)
        consts, rows, gains_spread, gains_done = ph.sem("consts"), ph.sem("rows"), ph.sem("gains_spread"), ph.sem("gains_done")
        queries = Stack(core, ph, 4, iq_bank)
        relu = [ph.sbuf(f"relu{i}", [P, GROUP]) for i in range(2)]
        k_hi_done, doubled, keys_turned, keys_copied = (
            ph.sem(n) for n in ("k_hi_done", "doubled", "keys_turned", "keys_copied"))
        dotted, rectified, added = ph.sem("dotted"), ph.sem("rectified"), ph.sem("score_added")
        lat_squared = ph.sem("lat_squared")
        T = SB * len(groups)
        KEYS_TILE, LAST = 2 * SB, 4 * SB
        units = []
        for b, n in seen.items():
            step = n if n <= GROUP else n // 2
            units += [(b, h, at, at + step) for h in range(8) for at in range(0, n, step)]
        first_slot = KEYS_TILE + SB + 4
        per_slot = -(-len(units) // (T - first_slot))
        first_block = min(seen)
        choose_from = first_slot - 2 + 2 * -(-len([x for x in units if x[0] < first_block + 2]) // (2 * per_slot))

        def slot(pair, c):
            if not first_slot <= pair < T:
                return range(0)
            n = 2 * per_slot
            first = (pair - first_slot) * per_slot
            return range(*(min(first + k * n // DC, len(units)) for k in (c, c + 1)))

        HALVES = 2 * len(seen)

        def half(i):
            return 2 * (units[i][0] - first_block) + units[i][1] // 4

        def starts_half(i):
            return i == 0 or half(i) != half(i - 1)

        def q_half(j):
            return heads_of(iq[:, first_block + j // 2, (j % 2) * 4 * HD:(j % 2 + 1) * 4 * HD])

        def before_same(i):
            same = [j for j in range(i) if units[j][0] == units[i][0] and units[j][2] == units[i][2]]
            return same[-1] + 1 if same else 0

        def units_before(j):
            return len([i for i in range(len(units)) if half(i) < j])

        with nc.Block() as block:
            @block.sync
            def _(sp):
                at = 0
                for name, n in parts:
                    sp.dma_start(row[:, at:at + n], t[name]).then_inc(rows, 16)
                    at += n
                for dst, name in ((cos, "cos64"), (sin, "sin64")):
                    sp.dma_start(dst[:, :, :], t[name]).then_inc(consts, 16)
                proj.sync(sp)

            @block.tensor
            def _(pe):
                pe.wait_ge(rows, 16 * len(parts))
                for at in range(0, row.shape[1], GROUP):
                    to = min(at + GROUP, row.shape[1])
                    ins = pe.matmul(rstd_psum[:, at:to], core.ones[0:1, :], row[:, at:to], start=True, stop=True)
                ins.then_inc(gains_spread, 1)
                norm.tensor(pe)

                def dot(i):
                    b, h, lo, hi = units[i]
                    j = half(i)
                    if i == 0:
                        queries.turn(pe, 0)
                    if starts_half(i):
                        pe.wait_ge(queries.copied, j + 1)
                        pe.wait_ge(keys_copied, b + 1)
                    if i >= 2:
                        pe.wait_ge(rectified, i - 1)
                    for part in range(2):
                        ins = pe.matmul(dots[i % 2][:, 0:hi - lo], queries.stack[:, j % 2, h % 4, :],
                                        keysT[:, part, lo:hi], start=part == 0, stop=part == 1)
                    ins.then_inc(dotted, 1)
                    if i - units_before(j) == 2 and j + 1 < HALVES:
                        queries.turn(pe, j + 1)

                for tile in range(T):
                    if tile % 2 == 0:
                        if tile >= len(banks):
                            heads.wait_taken(pe, tile + 1 - len(banks))
                        proj.tensor(pe, tile, lambda c: [dot(i) for i in slot(tile, c)])
                    b = tile - KEYS_TILE - 4
                    if 0 <= b < SB:
                        pe.wait_ge(doubled, b + 1)
                        if b >= 1:
                            pe.wait_ge(keys_copied, b)
                        for i in range(2):
                            ins = pe.transpose(keys_bank[:, i * P:(i + 1) * P],
                                               twice[:, b % 2, i].rearrange("p a w -> p (a w)").bitcast(F32), core.ident[:, :])
                        ins.then_inc(keys_turned, 1)
            @block.scalar
            def _(act):
                proj.split_hi(act, 0, 0)
                proj.split_hi(act, 0, 1)
                norm.scalar(act, lambda n: proj.split_hi(act, 0, n // 2 + 2) if n % 2 and n // 2 + 2 < DC else None)
                def copy_queries(j):
                    act.wait_ge(queries.turned, j + 1)
                    if j >= 2:
                        act.wait_ge(dotted, units_before(j - 1))
                    act.activation(queries.stack[:, j % 2], queries.source(), ACT.Copy).then_inc(queries.copied, 1)

                def rectify(i):
                    _, _, lo, hi = units[i]
                    j = half(i)
                    if i == 0:
                        queries.split_hi(act, 0, q_half(0))
                        copy_queries(0)
                    if starts_half(i) and j + 1 < HALVES:
                        queries.split_hi(act, j + 1, q_half(j + 1))
                    if i - units_before(j) == 3 and j + 1 < HALVES:
                        copy_queries(j + 1)
                    act.wait_ge(dotted, i + 1)
                    if i >= 2:
                        act.wait_ge(added, i - 1)
                    act.activation(relu[i % 2][:, 0:hi - lo], dots[i % 2][:, 0:hi - lo], ACT.Relu).then_inc(rectified, 1)

                def square_latents(b):
                    act.wait_ge(heads.copied, heads.copied_by[T - SB + b + 1])
                    for i, (lo, hi) in enumerate(((0, 256), (256, 384), (384, 416))):
                        if 3 * b + i:
                            act.wait_ge(lat_squared, 3 * b + i)
                        act.activation(heads.sq[0][:, 0:hi - lo], lat[:, b, lo:hi], ACT.Square,
                                       accum_out=lat_sum[:, i, b:b + 1]).then_inc(lat_squared, 1)

                for pair in range(0, T, 2):
                    for tile in (pair, pair + 1):
                        heads.scalar(act, tile)
                        b = tile - KEYS_TILE - 4
                        if 0 <= b < SB:
                            act.wait_ge(keys_turned, b + 1)
                            act.activation(keysT[:, :, b * P:(b + 1) * P],
                                           keys_bank[:, 0:2 * P].rearrange("p (h s) -> p h s", h=2), ACT.Copy)\
                               .then_inc(keys_copied, 1)
                        if tile >= T - SB:
                            square_latents(tile - (T - SB))
                    for c in range(DC):
                        if proj.ends_group(pair + 2):
                            proj.split_hi(act, (pair + 2) // SB + 1, c)
                        for i in slot(pair + 2, c):
                            rectify(i)

            @block.gpsimd
            def _(pool):
                proj.split_lo(pool, 0, 0)
                proj.split_lo(pool, 0, 1)
                norm.gpsimd(pool, lambda n: proj.split_lo(pool, 0, n // 2 + 2) if n // 2 + 2 < DC else None)
                pool.wait_ge(consts, 32)
                for pair in range(0, T, 2):
                    for tile in (pair, pair + 1):
                        heads.gpsimd(pool, tile)
                    for c in range(DC):
                        if proj.ends_group(pair + 2):
                            proj.split_lo(pool, (pair + 2) // SB + 1, c)
                        for i in slot(pair + 2, c):
                            if i == 0:
                                queries.split_lo(pool, 0, q_half(0))
                            if starts_half(i) and half(i) + 1 < HALVES:
                                queries.split_lo(pool, half(i) + 1, q_half(half(i) + 1))
                heads.gpsimd(pool, T)

            @block.vector
            def _(dve):
                dve.wait_ge(gains_spread, 1)
                dve.tensor_copy(gains[:, :], rstd_psum[:, 0:gains.shape[1]]).then_inc(gains_done, 1)
                dve.wait_ge(gains_done, 1)
                for i, name in enumerate(("e_dsa_qnorm", "e_mla_qnorm")):
                    dve.tensor_scalar(gain[name], gain[name], -1.0, None, ALU.mult).then_inc(gains_done, 1)
                norm.vector(dve)
                norm.wait_lo(dve, norm.UNITS - 1)
                dve.wait_ge(gains_done, 3)
                dve.wait_ge(consts, 32)
                def double_keys(b):
                    dve.wait_ge(heads.finished, heads.first[KEYS_TILE + b + 1])
                    if b >= 2:
                        dve.wait_ge(keys_turned, b - 1)
                    k = spread(keys[:, b, HD:2 * HD], 2)
                    dve.tensor_copy(twice[:, b % 2, 0], k).then_inc(k_hi_done, 1)
                    dve.wait_ge(k_hi_done, b + 1)
                    dve.tensor_tensor(twice[:, b % 2, 1], k, twice[:, b % 2, 0].bitcast(F32), ALU.subtract)\
                       .then_inc(doubled, 1)

                def add_score(i):
                    qb, h, lo, hi = units[i]
                    if starts_half(i):
                        dve.wait_ge(queries.lo_done, half(i) + 1)
                    dve.wait_ge(rectified, i + 1)
                    out, r, w = scores[qb][:, lo:hi], relu[i % 2][:, 0:hi - lo], iw[:, qb, h:h + 1]
                    if h == 0:
                        dve.tensor_scalar(out, r, w, None, ALU.mult).then_inc(added, 1)
                    else:
                        dve.wait_ge(added, before_same(i))
                        dve.scalar_tensor_tensor(out, r, w, out, ALU.mult, ALU.add).then_inc(added, 1)
                    if i + 1 == len(units) or units[i + 1][0] != qb:
                        topk.scored(dve, qb, added, i + 1)

                for pair in range(0, T, 2):
                    for tile in (pair, pair + 1):
                        heads.vector(dve, tile)
                        if 0 <= tile - 2 - KEYS_TILE < SB:
                            double_keys(tile - 2 - KEYS_TILE)
                    for c in range(DC):
                        for i in slot(pair + 2, c):
                            add_score(i)
                        if pair >= choose_from:
                            passed = pair - choose_from + 2 * (c + 1) / DC
                            topk.run(dve, rounds * passed / (T - choose_from))
                heads.vector(dve, T)
                heads.vector(dve, T + 1)


def latent_heads(core, t, group, lat, lat_sum, lat_rstd, turned_pe, gain, qT, kT, v):
    nc = core.nc
    H, QW = 4, 96
    with Phase(nc, f"latent_heads{group}") as ph:
        banks = [ph.psum(f"tile{i}", GROUP) for i in range(4)]
        lat_banks = [ph.psum(f"lat_bank{i}", GROUP) for i in range(2)]
        turn_banks = [ph.psum(f"turn_bank{i}", GROUP) for i in range(2)]
        NQ, NKV = H * QW, H * 2 * HD
        raw = ph.sbuf("raw", [P, 2 * NQ + NKV])
        cos32, sin32 = ph.sbuf("cos32", [P, SB, 32]), ph.sbuf("sin32", [P, SB, 32])
        consts = ph.sem("consts")
        w_hi, w_lo = ph.sbuf("w_hi", [P, 2 * NQ + NKV], F32R), ph.sbuf("w_lo", [P, 2 * NQ + NKV], F32R)
        lat_n = ph.sbuf("lat_n", [P, 2, 3 * P])
        lT_hi, lT_lo = ph.sbuf("lT_hi", [P, 2, 3, P], F32R), ph.sbuf("lT_lo", [P, 2, 3, P], F32R)
        q_n, k_n = ph.sbuf("q_n", [P, 3, H, QW]), ph.sbuf("k_n", [P, 3, H, QW])
        mean = ph.sbuf("lat_mean", [P, 3, SB])
        part_cos, part_sin = ph.sbuf("pe_cos", [P, SB, 32]), ph.sbuf("pe_sin", [P, SB, 32])
        loaded, whi_done, wlo_done = ph.sem("w_loaded"), ph.sem("w_hi_done"), ph.sem("w_lo_done")
        averaged, rooted, pe_gained, pe_cos_done, pe_sin_done, pe_done = (
            ph.sem(n) for n in ("lat_averaged", "lat_rooted", "pe_gained", "pe_cos_done", "pe_sin_done", "pe_done"))
        normed, lat_turned, lhi_done, llo_done, ready = (
            ph.sem(n) for n in ("lat_normed", "lat_turned", "l_hi_done", "l_lo_done", "ready"))
        q_turned, k_turned, q_copied, k_copied = (ph.sem(n) for n in ("q_turned", "k_turned", "q_copied", "k_copied"))
        padded = ph.sem("padded")
        tiles, copies = [], []
        for b in range(SB):
            q, k = q_n[:, b % 3], k_n[:, b % 3]
            bank = heads_of(banks[(2 * b) % 4][:, 0:NQ], QW)
            tiles.append([Item(bank, q, gain["e_mla_qnorm"], 1.0, QW * EPS, q[:, :, HD:QW], cos32[:, b, :], sin32[:, b, :])])
            tiles[-1][0].after = (q_turned, b - 2)
            copies.append([])
            bank = heads_of(banks[(2 * b + 1) % 4][:, 0:NKV], 2 * HD)
            tiles.append([Item(bank[:, :, 0:HD], k[:, :, 0:HD], gain["e_mla_knorm"][:, 0:HD], 1.0 / QW,
                               mean[:, 2, b:b + 1], shared=(k[:, :, HD:QW], turned_pe[:, b, :]))])
            tiles[-1][0].after = (k_turned, b - 2)
            copies.append([(bank[:, :, HD:2 * HD], heads_of(v[:, b, :]), 1.0)])
        heads = Heads(core, ph, tiles, copies, ready, NQ, H * 32)

        with nc.Block() as block:
            @block.sync
            def _(sp):
                for dst, name in ((cos32, "cos32"), (sin32, "sin32")):
                    sp.dma_start(dst[:, :, :], t[name]).then_inc(consts, 16)
                for i in range(2):
                    sp.dma_start(raw[:, i * NQ:(i + 1) * NQ], t["e_w_qb"][0][i * P:(i + 1) * P, group * NQ:(group + 1) * NQ])\
                      .then_inc(loaded, 16)
                sp.dma_start(raw[:, 2 * NQ:], t["e_w_kvb"][0][:, group * NKV:(group + 1) * NKV]).then_inc(loaded, 16)

            @block.scalar
            def _(act):
                act.wait_ge(loaded, 48)
                act.activation(w_hi[:, :], raw[:, :], ACT.Copy).then_inc(whi_done, 1)

                def split(b):
                    act.wait_ge(lat_turned, b + 1)
                    if b >= 2:
                        act.wait_ge(ready, 2 * (b - 1))
                    act.activation(lT_hi[:, b % 2], lat_banks[b % 2][:, 0:3 * P].rearrange("p (c s) -> p c s", c=3),
                                   ACT.Copy).then_inc(lhi_done, 1)

                def copy_turned(b):
                    for turned, i, dst, copied in ((q_turned, 0, qT, q_copied), (k_turned, 1, kT, k_copied)):
                        act.wait_ge(turned, b + 1)
                        act.activation(dst[0:QW, :, b * P:(b + 1) * P],
                                       turn_banks[i][0:QW, :].rearrange("p (c s) -> p c s", c=H), ACT.Copy)\
                           .then_inc(copied, 1)

                split(0)
                for b in range(SB):
                    if b + 1 < SB:
                        split(b + 1)
                    heads.scalar(act, 2 * b)
                    heads.scalar(act, 2 * b + 1)
                    if b >= 2:
                        copy_turned(b - 2)
                copy_turned(SB - 2)
                copy_turned(SB - 1)

            @block.gpsimd
            def _(pool):
                pool.wait_ge(consts, 32)
                pool.wait_ge(averaged, 3)
                pool.tensor_tensor(lat_rstd[:, :, :].rearrange("p a b -> p (a b)"), mean[:, 0:2, :].rearrange("p a b -> p (a b)"),
                                   core.minus_half[:, :], ALU.pow).then_inc(rooted, 1)
                if group == 0:
                    pool.wait_ge(pe_gained, 1)
                    pe_ = lat[:, :, 384:416]
                    pool.tensor_tensor(part_sin[:, :, 0:16], pe_[:, :, 16:32], sin32[:, :, 0:16], ALU.mult)
                    pool.tensor_tensor(part_sin[:, :, 16:32], pe_[:, :, 0:16], sin32[:, :, 16:32], ALU.mult)\
                        .then_inc(pe_sin_done, 1)
                pool.wait_ge(whi_done, 1)
                pool.tensor_tensor(w_lo[:, :], raw[:, :], w_hi[:, :].bitcast(F32), ALU.subtract).then_inc(wlo_done, 1)
                for tile in range(2 * SB + 1):
                    heads.gpsimd(pool, tile)

            @block.vector
            def _(dve):
                for i, n in enumerate((256, 128, QW)):
                    dve.tensor_scalar(mean[:, i, :], lat_sum[:, i, :], 1.0 / n, EPS, ALU.mult, ALU.add).then_inc(averaged, 1)
                dve.wait_ge(averaged, 3)
                dve.wait_ge(consts, 32)
                if group == 0:
                    pe_ = lat[:, :, 384:416]
                    dve.tensor_tensor(pe_, pe_, spread(gain["e_mla_knorm"][:, HD:QW], SB), ALU.mult).then_inc(pe_gained, 1)
                    dve.wait_ge(pe_gained, 1)
                    dve.tensor_tensor(part_cos[:, :, :], pe_, cos32[:, :, :], ALU.mult).then_inc(pe_cos_done, 1)

                def normalise(b):
                    if b >= 2:
                        dve.wait_ge(lat_turned, b - 1)
                    dve.scalar_tensor_tensor(lat_n[:, b % 2, 0:256], lat[:, b, 0:256], lat_rstd[:, 0, b:b + 1],
                                             gain["e_qa_norm"], ALU.mult, ALU.mult)
                    dve.scalar_tensor_tensor(lat_n[:, b % 2, 256:384], lat[:, b, 256:384], lat_rstd[:, 1, b:b + 1],
                                             gain["e_kva_norm"], ALU.mult, ALU.mult).then_inc(normed, 1)

                def rest(b):
                    dve.wait_ge(lhi_done, b + 1)
                    dve.tensor_tensor(lT_lo[:, b % 2], lat_banks[b % 2][:, 0:3 * P].rearrange("p (c s) -> p c s", c=3),
                                      lT_hi[:, b % 2].bitcast(F32), ALU.subtract).then_inc(llo_done, 1)

                for turned in (qT, kT):
                    dve.memset(turned[QW:P, :, :], 0.0).then_inc(padded, 1)
                dve.wait_ge(rooted, 1)
                normalise(0)
                normalise(1)
                if group == 0:
                    dve.wait_ge(pe_cos_done, 1)
                    dve.wait_ge(pe_sin_done, 1)
                    dve.tensor_tensor(turned_pe[:, :, :], part_cos[:, :, :], part_sin[:, :, :], ALU.add).then_inc(pe_done, 1)
                    dve.wait_ge(pe_done, 1)
                rest(0)
                for b in range(SB + 1):
                    if b + 1 < SB:
                        rest(b + 1)
                    if b + 2 < SB:
                        normalise(b + 2)
                    for tile in (2 * b, 2 * b + 1):
                        heads.vector(dve, tile)

            @block.tensor
            def _(pe):
                def turn_latents(b):
                    pe.wait_ge(normed, b + 1)
                    if b >= 2:
                        pe.wait_ge(llo_done, b - 1)
                    for i in range(3):
                        ins = pe.transpose(lat_banks[b % 2][:, i * P:(i + 1) * P], lat_n[:, b % 2, i * P:(i + 1) * P],
                                           core.ident[:, :])
                    ins.then_inc(lat_turned, 1)

                def turn_heads(b):
                    for src, bank, turned, copied, tile in ((q_n, turn_banks[0], q_turned, q_copied, 2 * b),
                                                            (k_n, turn_banks[1], k_turned, k_copied, 2 * b + 1)):
                        pe.wait_ge(heads.finished, heads.first[tile + 1])
                        if b:
                            pe.wait_ge(copied, b)
                        for i in range(H):
                            ins = pe.transpose(bank[0:QW, i * P:(i + 1) * P], src[:, b % 3, i, :], core.ident[:, :])
                        ins.then_inc(turned, 1)

                turn_latents(0)
                pe.wait_ge(wlo_done, 1)
                for b in range(SB):
                    if b + 1 < SB:
                        turn_latents(b + 1)
                    pe.wait_ge(llo_done, b + 1)
                    for tile in (2 * b, 2 * b + 1):
                        if tile >= 4:
                            heads.wait_taken(pe, tile - 4)
                        chunks = ((0, 0), (1, NQ)) if tile % 2 == 0 else ((2, 2 * NQ),)
                        n = NQ if tile % 2 == 0 else NKV
                        for i, (c, at) in enumerate(chunks):
                            ins = split_matmuls(pe, banks[tile % 4][:, 0:n], lT_hi[:, b % 2, c], lT_lo[:, b % 2, c],
                                                w_hi[:, at:at + n], w_lo[:, at:at + n], i == 0, i == len(chunks) - 1)
                        ins.then_inc(ready, 1)
                    if b >= 2:
                        turn_heads(b - 2)
                turn_heads(SB - 2)
                turn_heads(SB - 1)


def topk_attention(core, topk, scores, bq, bv, keys):
    nc = core.nc
    with Phase(nc, "topk_att") as ph:
        turned_bank = ph.psum("turned", S)
        queries = Stack(core, ph, 8, turned_bank)
        twice = ph.sbuf("k_twice", [P, 2, SB, 2, HD], F32R)
        kT = ph.sbuf("kT", [P, 2, S], F32R)
        rows = [[Unit([(queries.stack[:, b % 2, h, :], kT[:, part, 0:(b + 1) * P]) for part in range(2)],
                      [bv[:, c, :] for c in range(b + 1)], mask=scores.get(b)) for h in range(8)] for b in range(SB)]
        q_rows = [heads_of(bq[:, b, :]) for b in range(SB)]
        att = Attention(core, ph, rows, q_rows, turned=[turned_bank])
        masks, k_hi_done, k_doubled = ph.sem("masks"), ph.sem("k_hi_done"), ph.sem("k_doubled")
        k_turned, k_copied = ph.sem("k_turned"), ph.sem("k_copied")
        with nc.Block() as block:
            @block.tensor
            def _(pe):
                pe.wait_ge(k_doubled, 1)
                for part in range(2):
                    for b in range(SB):
                        ins = pe.transpose(att.scores[part][:, b * P:(b + 1) * P],
                                           twice[:, part, b].rearrange("p a w -> p (a w)").bitcast(F32), core.ident[:, :])
                    ins.then_inc(k_turned, 1)

                def before(u):
                    if u % 8 == 4 and u // 8 + 1 < SB:
                        att.wait_copied(pe, u - 2)
                        queries.turn(pe, u // 8 + 1)

                def after_score(u):
                    if u % 8 == 4 and u // 8 + 1 < SB:
                        pe.wait_ge(queries.copied, u // 8 + 2)

                queries.turn(pe, 0)
                pe.wait_ge(queries.copied, 1)
                pe.wait_ge(k_copied, 2)
                att.tensor(pe, before, after_score)

            @block.gpsimd
            def _(pool):
                for j in range(SB):
                    queries.split_lo(pool, j, q_rows[j])

            @block.scalar
            def _(act):
                def copy_queries(j):
                    act.wait_ge(queries.turned, j + 1)
                    if j >= 2:
                        act.wait_ge(att.scored, 8 * (j - 1))
                    act.activation(queries.stack[:, j % 2], queries.source(), ACT.Copy).then_inc(queries.copied, 1)

                def next_queries(u):
                    if u // 8 + 1 < SB and u % 8 == 0:
                        queries.split_hi(act, u // 8 + 1, q_rows[u // 8 + 1])
                    if u // 8 + 1 < SB and u % 8 == 4:
                        copy_queries(u // 8 + 1)

                queries.split_hi(act, 0, q_rows[0])
                for part in range(2):
                    act.wait_ge(k_turned, part + 1)
                    act.activation(kT[:, part, :], att.scores[part][:, :], ACT.Copy).then_inc(k_copied, 1)
                copy_queries(0)
                att.scalar(act, next_queries)

            @block.vector
            def _(dve):
                k = keys[:, :, 0:HD].unsqueeze(2).broadcast_to([P, SB, 2, HD])
                dve.tensor_copy(twice[:, 0], k).then_inc(k_hi_done, 1)
                dve.wait_ge(k_hi_done, 1)
                dve.tensor_tensor(twice[:, 1], k, twice[:, 0].bitcast(F32), ALU.subtract).then_inc(k_doubled, 1)
                early = topk.done // (4 * topk.per_pair)
                LAST = 8 * topk.blocks[2 * early]
                for pair in range(early):
                    topk.mask(dve, pair, masks)
                dve.wait_ge(masks, 2 * early)
                choose = topk.spread_over(dve, att.units[:LAST], topk.done / 4, topk.rounds)

                def behind(u):
                    choose(u)
                    if u == LAST - 1:
                        topk.mask(dve, early, masks)
                        dve.wait_ge(masks, 2 * early + 2)

                att.vector(dve, lambda u: choose(u, 0.5), behind)


def program(nc, t, out):
    Phase.retired = []
    with ExitStack() as stack:
        core = Core(nc, stack)
        cols = [t["e_norm"].rearrange("l (r p) -> (l r) p", p=P), t["o_norm"].rearrange("l (r p) -> (l r) p", p=P),
                t["f_norm"].rearrange("l (r p) -> (l r) p", p=P), t["f_conv_b"].rearrange("l (r p) -> (l r) p", p=P),
                t["f_conv_w"].rearrange("l j (r p) -> (l j r) p", p=P)]
        load(core, t["x"][0], cols, t["ident"])
        global_mixer(core, t)
        conv_ffn(core, 0, t["f_w_up"][0], t["f_w_down"][0])
        window_mixer(core, t)
        conv_ffn(core, 1, t["f_w_up"][1], t["f_w_down"][1], out[0])


def kernel(**inputs):
    import concourse.bacc as bacc
    from concourse.bass_utils import run_bass_kernel_spmd

    nc = bacc.Bacc("TRN2", target_bir_lowering=False, num_devices=1)
    arrays = {name: np.ascontiguousarray(a) for name, a in inputs.items()}
    arrays.update(shape_constants())
    aps = {n: nc.dram_tensor(f"in_{n}", a.shape, F32, kind="ExternalInput").ap() for n, a in arrays.items()}
    out = nc.dram_tensor("y_out", (1, S, D), F32, kind="ExternalOutput").ap()
    program(nc, aps, out)
    got = run_bass_kernel_spmd(nc, [{f"in_{n}": a for n, a in arrays.items()}], core_ids=[0])
    return got.results[0]["y_out"]
```
